# Optimizing a Trainium2 kernel written in Bass

```python
import math
import jax, jax.numpy as jnp
from jax import lax
import numpy as np

"""One inference step of a 2-layer YOCO-style hybrid decoder trunk.

Layer 0 (self path): RMSNorm -> S5 diagonal complex state-space mixer + GLU -> residual;
                     RMSNorm -> PEER product-key expert retrieval -> residual.
Shared K/V: RMSNorm(residual after layer 0) @ w_kv -> one set of GQA keys/values (NoPE).
Layer 1 (cross path): RMSNorm -> sliding-window (128) GQA with learned per-head sinks over
                     the shared K/V -> residual; RMSNorm -> PEER -> residual.
Final RMSNorm.

Inputs:  x_prompt (BATCH, SEQ, D_MODEL); x_sample (DEC_BATCH, DEC_SEQ, D_MODEL);
         state_ssm_re / state_ssm_im (DEPTH//2, DEC_BATCH, N_GROUPS, STATE_DIM);
         cache_k_win / cache_v_win (DEC_BATCH, WIN_BUF, N_KV_HEADS, HEAD_DIM), row j = position
         PAST_LEN - WIN_BUF + j.
Returns: (y_prompt (BATCH, SEQ, D_MODEL), y_sample (DEC_BATCH, DEC_SEQ, D_MODEL),
          ssm_re_prompt, ssm_im_prompt (DEPTH//2, BATCH, N_GROUPS, STATE_DIM),
          k_win_prompt, v_win_prompt (BATCH, WIN_BUF, N_KV_HEADS, HEAD_DIM),
          ssm_re_sample, ssm_im_sample (DEPTH//2, DEC_BATCH, N_GROUPS, STATE_DIM),
          k_win_sample, v_win_sample (DEC_BATCH, WIN_BUF, N_KV_HEADS, HEAD_DIM)).
"""

D_MODEL = 1024
BATCH = 1
SEQ = 512
DEPTH = 2
DEC_BATCH = 8
DEC_SEQ = 8
PAST_LEN = 2048
PAGE_SIZE = 128

N_A_LAYERS = DEPTH // 2
N_B_LAYERS = DEPTH - N_A_LAYERS
GROUP_SIZE = 16
N_GROUPS = D_MODEL // GROUP_SIZE
STATE_DIM = 64
HEAD_DIM = 64
N_Q_HEADS = D_MODEL // HEAD_DIM
N_KV_HEADS = max(1, N_Q_HEADS // 8)
Q_PER_KV = N_Q_HEADS // N_KV_HEADS
WINDOW = 128
WIN_BUF = min(WINDOW, PAST_LEN)
ATTN_SCALE = 1.0 / math.sqrt(HEAD_DIM)
PEER_HEADS = 8
N_KEYS = 128
N_EXPERTS = N_KEYS * N_KEYS
PEER_TOPK = 16
PEER_DKEY = 256
PEER_DHALF = PEER_DKEY // 2
PEER_BLOCK = 128
EPS = 1e-5

kernel_name = 'yoco_s5_swa_sink_peer_step'

def _rmsnorm(x, g):
    xf = x.astype(jnp.float32)
    r = lax.rsqrt(jnp.mean(xf * xf, axis=-1, keepdims=True) + EPS)
    return (xf * r * g.astype(jnp.float32)).astype(x.dtype)

def _s5_mixer(u, h0_re, h0_im, lam_re, lam_im, log_dt, b_re, b_im, c_re, c_im, d_skip, w_glu):
    N, L, Dm = u.shape
    f32 = jnp.float32
    uf = u.astype(f32).reshape(N, L, N_GROUPS, GROUP_SIZE)
    lr = lam_re.astype(f32)
    li = lam_im.astype(f32)
    dt = jnp.exp(log_dt.astype(f32))[:, None]
    mag = jnp.exp(lr * dt)
    ab_re = mag * jnp.cos(li * dt)
    ab_im = mag * jnp.sin(li * dt)
    den = lr * lr + li * li
    f_re = ((ab_re - 1.0) * lr + ab_im * li) / den
    f_im = (ab_im * lr - (ab_re - 1.0) * li) / den
    br = b_re.astype(f32)
    bi = b_im.astype(f32)
    bb_re = f_re[..., None] * br - f_im[..., None] * bi
    bb_im = f_re[..., None] * bi + f_im[..., None] * br
    bu_re = jnp.einsum('nlgj,gpj->nlgp', uf, bb_re)
    bu_im = jnp.einsum('nlgj,gpj->nlgp', uf, bb_im)
    hr0 = h0_re.astype(f32)
    hi0 = h0_im.astype(f32)
    bu_re = bu_re.at[:, 0].add(ab_re * hr0 - ab_im * hi0)
    bu_im = bu_im.at[:, 0].add(ab_re * hi0 + ab_im * hr0)
    a_re = jnp.broadcast_to(ab_re, (1, L, N_GROUPS, STATE_DIM))
    a_im = jnp.broadcast_to(ab_im, (1, L, N_GROUPS, STATE_DIM))

    def combine(e1, e2):
        a1r, a1i, b1r, b1i = e1
        a2r, a2i, b2r, b2i = e2
        return (a1r * a2r - a1i * a2i,
                a1r * a2i + a1i * a2r,
                a2r * b1r - a2i * b1i + b2r,
                a2r * b1i + a2i * b1r + b2i)

    _, _, hr, hi = lax.associative_scan(combine, (a_re, a_im, bu_re, bu_im), axis=1)
    y = (jnp.einsum('nlgp,gjp->nlgj', hr, c_re.astype(f32))
         - jnp.einsum('nlgp,gjp->nlgj', hi, c_im.astype(f32))
         + d_skip.astype(f32).reshape(N_GROUPS, GROUP_SIZE) * uf)
    z = jax.nn.gelu(y.reshape(N, L, Dm), approximate=False)
    zz = z @ w_glu.astype(f32)
    out = zz[..., :Dm] * jax.nn.sigmoid(zz[..., Dm:])
    return out.astype(u.dtype), hr[:, -1].astype(u.dtype), hi[:, -1].astype(u.dtype)

def _prompt_context(k, v):
    N, L = k.shape[:2]
    nb = L // WINDOW
    kb = k.reshape(N, nb, WINDOW, N_KV_HEADS, HEAD_DIM)
    vb = v.reshape(N, nb, WINDOW, N_KV_HEADS, HEAD_DIM)
    kprev = jnp.concatenate([jnp.zeros_like(kb[:, :1]), kb[:, :-1]], axis=1)
    vprev = jnp.concatenate([jnp.zeros_like(vb[:, :1]), vb[:, :-1]], axis=1)
    k_ctx = jnp.concatenate([kprev, kb], axis=2)
    v_ctx = jnp.concatenate([vprev, vb], axis=2)
    i = jnp.arange(WINDOW)[None, :, None]
    j = jnp.arange(2 * WINDOW)[None, None, :]
    blk = jnp.arange(nb)[:, None, None]
    d = i + WINDOW - j
    mask = (d >= 0) & (d < WINDOW) & (blk * WINDOW + j - WINDOW >= 0)
    return (k_ctx, v_ctx, mask, k[:, L - WIN_BUF:], v[:, L - WIN_BUF:])

def _sample_context(k, v, k_buf, v_buf):
    L = k.shape[1]
    k_all = jnp.concatenate([k_buf.astype(k.dtype), k], axis=1)
    v_all = jnp.concatenate([v_buf.astype(v.dtype), v], axis=1)
    kpos = jnp.concatenate([PAST_LEN - WIN_BUF + jnp.arange(WIN_BUF), PAST_LEN + jnp.arange(L)])
    qpos = PAST_LEN + jnp.arange(L)
    d = qpos[:, None] - kpos[None, :]
    mask = ((d >= 0) & (d < WINDOW))[None]
    return (k_all[:, None], v_all[:, None], mask, k_all[:, -WIN_BUF:], v_all[:, -WIN_BUF:])

def _window_attention(q, k_ctx, v_ctx, mask, sinks):
    N, L = q.shape[:2]
    nb, qb, kb = mask.shape
    qbk = q.reshape(N, nb, qb, N_KV_HEADS, Q_PER_KV, HEAD_DIM)
    s = jnp.einsum('nbqkgd,nbjkd->nbkgqj', qbk, k_ctx).astype(jnp.float32) * ATTN_SCALE
    s = jnp.where(mask[None, :, None, None], s, -jnp.inf)
    sink = sinks.astype(jnp.float32).reshape(1, 1, N_KV_HEADS, Q_PER_KV, 1, 1)
    m = jnp.maximum(jnp.max(s, axis=-1, keepdims=True), sink)
    e = jnp.exp(s - m)
    w = e / (jnp.sum(e, axis=-1, keepdims=True) + jnp.exp(sink - m))
    o = jnp.einsum('nbkgqj,nbjkd->nbqkgd', w.astype(v_ctx.dtype), v_ctx)
    return o.reshape(N, L, N_Q_HEADS * HEAD_DIM)

def _peer(x, w_q, sub_keys, u_tab, v_tab):
    N, L, Dm = x.shape
    T = N * L
    nblk = -(-T // PEER_BLOCK)
    t = jnp.pad(x.reshape(T, Dm), ((0, nblk * PEER_BLOCK - T), (0, 0)))
    t = t.reshape(nblk, PEER_BLOCK, Dm)
    sk = sub_keys.astype(jnp.float32)

    def one(xb):
        q = (xb @ w_q).astype(jnp.float32).reshape(PEER_BLOCK, PEER_HEADS, 2, PEER_DHALF)
        s = jnp.einsum('bhcd,hcnd->bhcn', q, sk)
        sv, si = lax.top_k(s, PEER_TOPK)
        cand = (sv[:, :, 0, :, None] + sv[:, :, 1, None, :]).reshape(PEER_BLOCK, PEER_HEADS, PEER_TOPK * PEER_TOPK)
        cid = (si[:, :, 0, :, None] * N_KEYS + si[:, :, 1, None, :]).reshape(PEER_BLOCK, PEER_HEADS, PEER_TOPK * PEER_TOPK)
        fv, fi = lax.top_k(cand, PEER_TOPK)
        eid = jnp.take_along_axis(cid, fi, axis=-1)
        g = jax.nn.softmax(fv, axis=-1)
        hpre = jnp.einsum('bd,bhkd->bhk', xb, u_tab[eid])
        a = (jax.nn.gelu(hpre.astype(jnp.float32), approximate=False) * g).astype(xb.dtype)
        return jnp.einsum('bhk,bhkd->bd', a, v_tab[eid])

    out = lax.map(one, t).reshape(nblk * PEER_BLOCK, Dm)[:T]
    return out.reshape(N, L, Dm).astype(x.dtype)

def _trunk(x, h0_re, h0_im, k_buf, v_buf, p):
    N, L, _ = x.shape
    h = x
    fin_re = []
    fin_im = []
    ctx = None
    for layer in range(DEPTH):
        if layer < N_A_LAYERS:
            a = layer
            y, sr, si = _s5_mixer(_rmsnorm(h, p['norm_mix'][layer]), h0_re[a], h0_im[a],
                                  p['ssm_lam_re'][a], p['ssm_lam_im'][a], p['ssm_log_dt'][a],
                                  p['ssm_b_re'][a], p['ssm_b_im'][a], p['ssm_c_re'][a], p['ssm_c_im'][a],
                                  p['ssm_d'][a], p['ssm_w_glu'][a])
            fin_re.append(sr)
            fin_im.append(si)
            h = h + y
        else:
            if ctx is None:
                kv = (_rmsnorm(h, p['norm_kv']) @ p['w_kv']).reshape(N, L, 2, N_KV_HEADS, HEAD_DIM)
                k, v = kv[:, :, 0], kv[:, :, 1]
                if k_buf is None:
                    ctx = _prompt_context(k, v)
                else:
                    ctx = _sample_context(k, v, k_buf, v_buf)
            b = layer - N_A_LAYERS
            q = (_rmsnorm(h, p['norm_mix'][layer]) @ p['w_q'][b]).reshape(N, L, N_KV_HEADS, Q_PER_KV, HEAD_DIM)
            o = _window_attention(q, ctx[0], ctx[1], ctx[2], p['attn_sinks'][b])
            h = h + o @ p['w_o'][b]
        h = h + _peer(_rmsnorm(h, p['norm_ffn'][layer]), p['peer_w_q'][layer], p['peer_sub_keys'][layer],
                      p['peer_u'][layer], p['peer_v'][layer])
    y = _rmsnorm(h, p['norm_final'])
    return y, jnp.stack(fin_re), jnp.stack(fin_im), ctx[3], ctx[4]

def setup_inputs(seed: int = 0) -> dict:
    key = jax.random.key(seed)
    ks = list(jax.random.split(key, 32))
    f32 = jnp.float32

    def nrm(i, shape, scale):
        return jax.random.normal(ks[i], shape, f32) * scale

    n_pos = jnp.pi * jnp.arange(STATE_DIM, dtype=f32)
    return {
        'x_prompt': nrm(0, (BATCH, SEQ, D_MODEL), 1.0),
        'x_sample': nrm(1, (DEC_BATCH, DEC_SEQ, D_MODEL), 1.0),
        'state_ssm_re': nrm(2, (N_A_LAYERS, DEC_BATCH, N_GROUPS, STATE_DIM), 0.1),
        'state_ssm_im': nrm(3, (N_A_LAYERS, DEC_BATCH, N_GROUPS, STATE_DIM), 0.1),
        'cache_k_win': nrm(4, (DEC_BATCH, WIN_BUF, N_KV_HEADS, HEAD_DIM), 1.0),
        'cache_v_win': nrm(5, (DEC_BATCH, WIN_BUF, N_KV_HEADS, HEAD_DIM), 1.0),
        'norm_mix': 1.0 + nrm(6, (DEPTH, D_MODEL), 0.02),
        'norm_ffn': 1.0 + nrm(7, (DEPTH, D_MODEL), 0.02),
        'norm_kv': 1.0 + nrm(8, (D_MODEL,), 0.02),
        'norm_final': 1.0 + nrm(9, (D_MODEL,), 0.02),
        'ssm_lam_re': -0.5 + nrm(10, (N_A_LAYERS, N_GROUPS, STATE_DIM), 0.01),
        'ssm_lam_im': n_pos + nrm(11, (N_A_LAYERS, N_GROUPS, STATE_DIM), 0.01),
        'ssm_log_dt': jax.random.uniform(ks[12], (N_A_LAYERS, N_GROUPS), f32, math.log(1e-3), math.log(1e-1)),
        'ssm_b_re': nrm(13, (N_A_LAYERS, N_GROUPS, STATE_DIM, GROUP_SIZE), (2 * GROUP_SIZE) ** -0.5),
        'ssm_b_im': nrm(14, (N_A_LAYERS, N_GROUPS, STATE_DIM, GROUP_SIZE), (2 * GROUP_SIZE) ** -0.5),
        'ssm_c_re': nrm(15, (N_A_LAYERS, N_GROUPS, GROUP_SIZE, STATE_DIM), 1.0),
        'ssm_c_im': nrm(16, (N_A_LAYERS, N_GROUPS, GROUP_SIZE, STATE_DIM), 1.0),
        'ssm_d': nrm(17, (N_A_LAYERS, D_MODEL), 1.0),
        'ssm_w_glu': nrm(18, (N_A_LAYERS, D_MODEL, 2 * D_MODEL), D_MODEL ** -0.5),
        'w_kv': nrm(19, (D_MODEL, 2 * N_KV_HEADS * HEAD_DIM), D_MODEL ** -0.5),
        'w_q': nrm(20, (N_B_LAYERS, D_MODEL, N_Q_HEADS * HEAD_DIM), D_MODEL ** -0.5),
        'attn_sinks': nrm(21, (N_B_LAYERS, N_Q_HEADS), 0.5),
        'w_o': nrm(22, (N_B_LAYERS, N_Q_HEADS * HEAD_DIM, D_MODEL), (N_Q_HEADS * HEAD_DIM) ** -0.5),
        'peer_w_q': nrm(23, (DEPTH, D_MODEL, PEER_HEADS * PEER_DKEY), D_MODEL ** -0.5),
        'peer_sub_keys': nrm(24, (DEPTH, PEER_HEADS, 2, N_KEYS, PEER_DHALF), PEER_DHALF ** -0.5),
        'peer_u': nrm(25, (DEPTH, N_EXPERTS, D_MODEL), D_MODEL ** -0.5),
        'peer_v': nrm(26, (DEPTH, N_EXPERTS, D_MODEL), 0.1),
    }

def reference(x_prompt, x_sample, state_ssm_re, state_ssm_im, cache_k_win, cache_v_win,
              norm_mix, norm_ffn, norm_kv, norm_final,
              ssm_lam_re, ssm_lam_im, ssm_log_dt, ssm_b_re, ssm_b_im, ssm_c_re, ssm_c_im, ssm_d, ssm_w_glu,
              w_kv, w_q, attn_sinks, w_o,
              peer_w_q, peer_sub_keys, peer_u, peer_v):
    p = {'norm_mix': norm_mix, 'norm_ffn': norm_ffn, 'norm_kv': norm_kv, 'norm_final': norm_final,
         'ssm_lam_re': ssm_lam_re, 'ssm_lam_im': ssm_lam_im, 'ssm_log_dt': ssm_log_dt,
         'ssm_b_re': ssm_b_re, 'ssm_b_im': ssm_b_im, 'ssm_c_re': ssm_c_re, 'ssm_c_im': ssm_c_im,
         'ssm_d': ssm_d, 'ssm_w_glu': ssm_w_glu, 'w_kv': w_kv, 'w_q': w_q, 'attn_sinks': attn_sinks,
         'w_o': w_o, 'peer_w_q': peer_w_q, 'peer_sub_keys': peer_sub_keys, 'peer_u': peer_u, 'peer_v': peer_v}
    z0 = jnp.zeros((N_A_LAYERS, x_prompt.shape[0], N_GROUPS, STATE_DIM), x_prompt.dtype)
    y_prompt, sre_p, sim_p, kw_p, vw_p = _trunk(x_prompt, z0, z0, None, None, p)
    y_sample, sre_s, sim_s, kw_s, vw_s = _trunk(x_sample, state_ssm_re, state_ssm_im, cache_k_win, cache_v_win, p)
    return (y_prompt, y_sample, sre_p, sim_p, kw_p, vw_p, sre_s, sim_s, kw_s, vw_s)


_drawn_inputs = setup_inputs


def setup_inputs(seed=0):
    import zlib

    import numpy as np

    out = dict(_drawn_inputs(seed))
    spreads = {}
    factors = {'norm_mix': 2.676,
     'norm_ffn': 5.6,
     'norm_kv': 2.987,
     'norm_final': 8.175,
     'ssm_lam_re': 3.978,
     'attn_sinks': 27.316}
    for name, (base, spread) in spreads.items():
        noise = np.random.default_rng([zlib.crc32(name.encode()), seed]).standard_normal(out[name].shape)
        drawn = base * np.exp(spread * noise) if base else spread * noise
        out[name] = __import__('jax').numpy.asarray(drawn.astype(out[name].dtype))
    for name, factor in factors.items():
        out[name] = (out[name] * factor).astype(out[name].dtype)
    return out
```

```python
from contextlib import ExitStack

import concourse.bass as bass
from concourse import mybir

ALU = mybir.AluOpType
ACT = mybir.ActivationFunctionType
AX = mybir.AxisListType
F32 = mybir.dt.float32
BF16 = mybir.dt.bfloat16
I32 = mybir.dt.int32
U32 = mybir.dt.uint32

P = 128
D = 1024
KT = D // P
SEQ, NSEQ, STEPS = 512, 8, 8
TOK = SEQ + NSEQ * STEPS
FULL = SEQ // P
TILES = FULL + 1
LAST = TOK - SEQ
Q = 8
CH = SEQ // Q
NC = CH + NSEQ
G, GS, SD = 64, 16, 64
PAIRS = G // 2
BLK = Q * GS
HEADS, NKEY, TOPK = 8, 128, 16
QH, KVH, HD = 16, 2, 64
QPK = QH // KVH
WIDE = P + LAST
SCALE = HD ** -0.5
EPS = 1e-5
NEG = -1.0e30
LOWEST = -3.0e38
PI = 3.141592653589793


class Chain:

    def __init__(self, eng, sem):
        self.eng, self.sem, self.n = eng, sem, 0

    def __call__(self, ins):
        ins.then_inc(self.sem, 1)
        self.n += 1
        self.eng.wait_ge(self.sem, self.n)

    def reset(self):
        self.eng.sem_clear(self.sem)
        self.n = 0


NU_RING, NV_RING = 8, 4


def gate(eng, sem, value):
    if isinstance(value, int):
        if value > 0:
            eng.wait_ge(sem, value)
    else:
        eng.wait_ge(sem, value)
        eng.nop(nofuse=True)


class LayerSems:

    def __init__(self, sems, counts, layer):
        self.sems, self.counts, self.layer = sems, counts, layer

    def __getitem__(self, name):
        return self.sems[name]

    def value(self, name, n):
        return n + self.layer * self.counts[name]

    def wait(self, eng, name, n):
        gate(eng, self.sems[name], self.value(name, n))


def build(nc, io):
    with ExitStack() as ctx:
        def sb(name, shape, dt=F32):
            return ctx.enter_context(nc.sbuf_tensor(name, shape, dt))

        def sem(name):
            return ctx.enter_context(nc.semaphore(name))

        arena = sb("arena", [P, 47616])

        def area(start, *shape):
            n = 1
            for k in shape:
                n *= k
            flat = arena[:, start:start + n]
            if len(shape) == 1:
                return flat
            names = "abcd"[:len(shape)]
            return flat.rearrange(f"p ({' '.join(names)}) -> p {' '.join(names)}",
                                  **dict(zip(names[1:], shape[1:])))

        X = area(0, Q, D)
        M = area(0, G, Q * GS)
        Z = area(0, Q, D)
        U = area(8192, G, NC)
        ZT = area(8192, KT, TOK)
        XN = area(12800, G, Q, GS)
        E = area(12800, 2, PAIRS, BLK)
        K = area(12800, G, BLK)
        WIN = area(20992, PAIRS, 2, 2, SD)
        CA = area(29184, 2, PAIRS, Q + 1, GS)
        HP = area(38400, 2, PAIRS, NC)
        TMP = area(38400, PAIRS * (Q + 1) * GS)
        V = area(43008, 2, PAIRS, NC)
        BRAW = area(43008, 2, PAIRS, GS)
        CRAW = area(44032, 2, PAIRS, GS)
        GAIN0 = area(45056, D)
        SQ = area(46080, D)
        WGLU = area(12800, KT, 2 * D)
        H = area(38400, TILES, D)
        SG = area(43520, 2, D)

        WQ = [area(0, KT // 2, 2 * D), area(29184, KT // 2, 2 * D)]
        UROWS = area(8192, NU_RING, D)
        VROWS = area(16384, NV_RING, D)
        XCUR = area(20480, D)
        XNEXT = area(21504, D)
        XT = area(22528, KT, P)
        GAIN = area(23552, D)
        GAINF = area(0, D)
        YSQ = area(1024, D)
        SC = area(24576, 2, 2, NKEY)
        SC2 = area(25088, 2, NKEY)
        QN = area(25600, 2, 2 * P)
        QT = area(26112, 2, 2, P)
        CAND, CAND2 = area(26624, TOPK, TOPK), area(26880, TOPK, TOPK)
        EQ = area(27136, 2, TOPK, TOPK)
        FV = area(27648, HEADS, TOPK)
        EXPS = area(27776, HEADS, TOPK)
        GATE = area(28160, TILES * P)
        EID = area(37376, TILES * P).bitcast(U32)
        JUNK = area(43520, D).bitcast(BF16).rearrange("p (a b) -> p a b", a=2)
        DIAG = area(44544, 4, P)
        KEYS = area(45568, 2 * HEADS, NKEY)

        WQA = area(0, KT, D)
        WO = area(29184, KT, D)
        WKV = area(8192, KT, 2 * P)
        PB = area(10240, QPK, KVH, 2 * P)
        PT = area(14336, 2, QPK, KVH, P)
        SB = area(10240, NSEQ, WIDE)
        VBUF, KBUF = area(11776, NSEQ, P), area(12800, NSEQ, P)
        PTB, PTN = area(14336, NSEQ, P), area(15360, NSEQ, P)
        QBD, KBT = area(16384, NSEQ, P), area(17408, NSEQ, P)
        GKV, GMX = area(18432, D), area(19456, D)
        XK, XQ = area(20480, D), area(21504, D)
        XKT, XQT = area(22528, KT, P), area(23552, KT, P)
        QTA, QNA = area(24576, QPK, P), area(25600, D)
        OT = area(26624, QPK, P)
        KVN = area(27648, 2 * P)
        KZ = area(43520, KVH, P + TOK)
        V2 = area(44928, 2, P)
        KNT = area(45184, LAST)
        MASKS = area(45568, 2 * 2 * P)
        MASK1, MASKN = MASKS[:, 0:2 * P], MASKS[:, 2 * P:4 * P]
        SMASK = area(46080, NSEQ, WIDE)
        sinks = sb("sinks", [P, QPK * KVH + 1])
        mx = sb("mx", [P, 4, QH])

        top = sb("top", [P, 2, TOPK])
        topi = sb("topi", [P, 2, TOPK], U32)
        best_v = sb("best_v", [P, TOPK])
        best_i = sb("best_i", [P, TOPK], U32)
        ab = sb("ab", [P, 2, TOPK], U32)
        picked = sb("picked", [P, 2, TOPK])
        iota = sb("iota", [P, TOPK])
        idxu = sb("idxu", [P, 2, TOPK], U32)
        idxv = sb("idxv", [P, 2, TOPK], U32)
        hp = sb("hp", [P, 2, TOPK])
        ge = sb("ge", [P, 2, TOPK])
        av = sb("av", [P, 2, TOPK])
        sums = sb("sums", [P, 2, HEADS])
        rt = sb("rt", [P, 4])

        ident = sb("ident", [P, P])
        par = sb("par", [P, 3, PAIRS])
        w = sb("w", [P, 16, PAIRS])
        wi = sb("wi", [P, PAIRS], I32)
        pw = sb("pw", [P, 2, Q + 1, PAIRS])
        pwr = sb("pwr", [P, 2, Q, PAIRS])
        Bb = sb("Bb", [P, 2, PAIRS, GS])
        a8 = sb("a8", [P, 2, 2, PAIRS])
        pr8 = sb("pr8", [P, 2, 2, PAIRS])
        h0 = sb("h0", [P, 2, NSEQ, PAIRS])
        hs = sb("hs", [P, 2, NSEQ, PAIRS])
        hf = sb("hf", [P, 2, PAIRS])
        dsk = sb("dsk", [GS, G])
        zero = sb("zero", [GS, (Q - 1) * GS])
        st = sb("st", [P, 4, Q])

        ps = ctx.enter_context(nc.psum_tensor("ps", [P, 8, 512], F32))

        x_in, gain_in, par_in = sem("x_in"), sem("gain_in"), sem("par_in")
        bc_in, ident_in, pad_out = sem("bc_in"), sem("ident_in"), sem("pad_out")
        squares, roots_in, roots = sem("squares"), sem("roots_in"), sem("roots")
        normed, angles, sines = sem("normed"), sem("angles"), sem("sines")
        e_ready, ca_ready, zeroed = sem("e_ready"), sem("ca_ready"), sem("zeroed")
        turned, turned_out = sem("turned"), sem("turned_out")
        skip_added, m_out, k_in = sem("skip_added"), sem("m_out"), sem("k_in")
        v_ready, v_act, v_dve = sem("v_ready"), sem("v_act"), sem("v_dve")
        scanned, y_ready, y_out = sem("scanned"), sem("y_ready"), sem("y_out")
        z_ready, z_act, z_dve = sem("z_ready"), sem("z_act"), sem("z_dve")
        glu_in, h_in, glu_ready = sem("glu_in"), sem("h_in"), sem("glu_ready")
        gate_ready, mixed = sem("gate_ready"), sem("mixed")
        states_out, state_ready = sem("states_out"), sem("state_ready")
        s_dve, s_act = sem("s_dve"), sem("s_act")
        wq_in, iota_in, sinks_in, gainf_in = sem("wq_in"), sem("iota_in"), sem("sinks_in"), sem("gainf_in")
        wa_in, wkv_in, buf_in, win_out = sem("wa_in"), sem("wkv_in"), sem("buf_in"), sem("win_out")
        y_ready2, y_stored = sem("y_ready2"), sem("y_stored")
        att_names = ("ms root x xt xt_copied kv kv_copied kt kt_copied q q_copied qt qt_copied s masked "
                     "max exps probs pt pt_act pt_dve o o_copied y added").split()
        att_sems = [{n: sem(f"{n}_{k}") for n in att_names} for k in ("prompt", "sample")]
        sample_q = sem("sample_q")
        last_ms, last_root = sem("last_ms"), sem("last_root")
        per_tile = "ms_ready root_ready x_ready x_cur xt_ready fv_ready exp_done gated h_done".split()
        per_head = ("q_ready q_copied qt_ready qt_copied sc_ready sc_copied routed idxu_ready idxv_ready "
                    "gelus weights").split()
        counts = {"xt_copied": 2 * TILES, **dict.fromkeys(per_tile, TILES), **dict.fromkeys(per_head, HEADS * TILES),
                  **dict.fromkeys(("dots", "diags", "products"), TOPK * HEADS * TILES)}
        peer_sem = {n: sem(n) for n in counts}
        peer_sems = [LayerSems(peer_sem, counts, layer) for layer in range(2)]
        u_in = [sem(f"u_in{i}") for i in range(NU_RING)]
        v_in = [sem(f"v_in{i}") for i in range(NV_RING)]

        UR = [list(range(7 * r, min(7 * r + 7, G))) for r in range(-(-G // 7))]
        WR = [(ri, 4 * r) for ri in range(2) for r in range(PAIRS // 4)]
        NU, NW = len(UR), len(WR)
        PR = PAIRS // 4
        VR = [list(range(6 * r, min(6 * r + 6, PAIRS))) for r in range(-(-PAIRS // 6))]

        def v_copy(copy, r, pairs, ri, g2):
            n = len(pairs)
            b = 2 * (r % 4)
            half = n // 2
            src = ps[SD * ri:SD * ri + SD, b:b + 2, 0:half * 2 * NC].rearrange(
                "p a (q g n) -> p a q g n", g=2, n=NC)[:, :, :, g2, :]
            dst = V[SD * g2:SD * g2 + SD, ri, pairs[0]:pairs[0] + n, :].rearrange("p (a q) n -> p a q n", a=2)
            return copy(dst, src)

        def pt_copy(copy, r):
            return copy(PT[:, :, r, :, :], ps[:, r, :].rearrange("p (h k n) -> p h k n", h=2, k=2))

        def z_copy(copy, r):
            kt, half = r // 2, r % 2
            dst = ZT[:, kt, :].rearrange("p (c s) -> p s c", s=Q)[:, 4 * half:4 * half + 4, :]
            return copy(dst, ps[:, r % 4, 0:4 * NC].rearrange("p (s c) -> p s c", c=NC))

        block = ctx.enter_context(nc.Block())

        @block.sync
        def _(sp):
            sp.dma_start(ident[:, :], io["ident"]).then_inc(ident_in, 16)
            sp.dma_start(arena[0:NC, 0:Q * D], io["x"].rearrange("(c s) d -> c (s d)", s=Q)).then_inc(x_in, 16)
            sp.dma_start(GAIN0, io["gains"][0:1, :].partition_broadcast(P)).then_inc(gain_in, 16)
            sp.dma_start(par[:, :, :], io["s5par"]).then_inc(par_in, 16)
            sp.dma_start(BRAW, io["s5b"]).then_inc(bc_in, 16)
            sp.dma_start(CRAW, io["s5c"]).then_inc(bc_in, 16)
            sp.dma_start(h0[:, :, :, :], io["h0"]).then_inc(bc_in, 16)
            sp.dma_start(dsk[:, :], io["dskip"]).then_inc(bc_in, 16)
            sp.wait_ge(zeroed, 1)
            mp = io["kern"].rearrange("g j n -> j g n")
            sp.dma_start(mp[:, :, 0:(Q - 1) * GS],
                         zero[:, :].unsqueeze(1).to_broadcast([GS, G, (Q - 1) * GS])).then_inc(pad_out, 16)
            sp.wait_ge(skip_added, 1)
            sp.dma_start(mp[:, :, (Q - 1) * GS:], M[0:GS, :, :]).then_inc(m_out, 16)
            sp.wait_ge(pad_out, 16)
            sp.wait_ge(m_out, 16)
            sp.wait_ge(turned, NU + NW)
            for s in range(Q):
                a = (Q - 1 - s) * GS
                sp.dma_start(K[GS * s:GS * s + GS, :, :], mp[:, :, a:a + BLK]).then_inc(k_in, 16)
            glu = io["w_glu"].rearrange("(k p) n -> p k n", p=P)
            sp.wait_ge(v_ready, len(VR))
            sp.dma_start(WGLU[:, 4:8, :], glu[:, 4:8, :]).then_inc(glu_in, 16)
            sp.wait_ge(state_ready, 2)
            sp.dma_start(io["hs"], hs[:, :, :, :]).then_inc(states_out, 16)
            sp.dma_start(io["hf"], hf[:, :, :]).then_inc(states_out, 16)
            sp.wait_ge(y_ready, PR)
            sp.dma_start(WGLU[:, 0:4, :], glu[:, 0:4, :]).then_inc(glu_in, 16)
            sp.dma_start(H[:, 0:FULL, :], io["x"][0:SEQ, :].rearrange("(t p) d -> p t d", p=P)).then_inc(h_in, 16)
            sp.dma_start(H[0:LAST, FULL, :], io["x"][SEQ:TOK, :]).then_inc(h_in, 16)
            sp.dma_start(iota[:, :], io["iota"]).then_inc(iota_in, 16)
            wq = io["peer_wq"]
            sp.wait_ge(z_ready, 2 * KT)
            for i in range(2):
                sp.dma_start(WQ[i], wq[0].rearrange("(k p) n -> p k n", p=P)[:, 4 * i:4 * i + 4, :]).then_inc(wq_in, 16)
            sp.wait_ge(mixed, TILES)
            sp.dma_start(GAIN, io["gains"][2:3, :].partition_broadcast(P)).then_inc(wq_in, 16)
            sp.dma_start(KEYS, io["keys"][0]).then_inc(wq_in, 16)
            sp.dma_start(sinks[:, :], io["sinks"]).then_inc(sinks_in, 16)
            S = peer_sems[0]
            S.wait(sp, "q_ready", HEADS * TILES)
            sp.dma_start(WQA, io["w_q"].rearrange("(k p) n -> p k n", p=P)).then_inc(wa_in, 16)
            sp.dma_start(WO, io["w_o"].rearrange("(k p) n -> p k n", p=P)).then_inc(wa_in, 16)
            S.wait(sp, "sc_ready", HEADS * TILES)
            sp.dma_start(MASKS, io["masks"]).then_inc(wa_in, 16)
            sp.dma_start(SMASK, io["smask"]).then_inc(wa_in, 16)
            S.wait(sp, "h_done", TILES)
            sp.dma_start(WKV, io["w_kv"].rearrange("(k p) n -> p k n", p=P)).then_inc(wkv_in, 16)
            sp.dma_start(GKV, io["gains"][4:5, :].partition_broadcast(P)).then_inc(wkv_in, 16)
            sp.dma_start(GMX, io["gains"][1:2, :].partition_broadcast(P)).then_inc(wkv_in, 16)
            sp.dma_start(io["kv_s"][0, :, 0:P - STEPS, :], io["k_buf"][:, STEPS:P, :]).then_inc(win_out, 16)
            sp.dma_start(io["kv_s"][1, :, 0:P - STEPS, :], io["v_buf"][:, STEPS:P, :]).then_inc(win_out, 16)
            A, B = att_sems
            sp.wait_ge(A["kv_copied"], 2 * FULL)
            sp.dma_start(io["kv_p"], KVN).then_inc(win_out, 16)
            sp.wait_ge(A["added"], FULL)
            sp.dma_start(KBUF, io["k_buf"].rearrange("b j n -> j b n")).then_inc(buf_in, 16)
            sp.dma_start(VBUF, io["v_buf"].rearrange("b j n -> j b n")).then_inc(buf_in, 16)
            sp.wait_ge(B["kv_copied"], 2)
            for i in range(2):
                sp.dma_start(io["kv_s"][i, :, P - STEPS:P, :], KVN[0:LAST, i * P:(i + 1) * P]).then_inc(win_out, 16)
            sp.wait_ge(B["q"], 1)
            sp.dma_start(WQ[0], wq[1].rearrange("(k p) n -> p k n", p=P)[:, 0:4, :]).then_inc(wq_in, 16)
            sp.wait_ge(B["y"], 1)
            sp.dma_start(WQ[1], wq[1].rearrange("(k p) n -> p k n", p=P)[:, 4:8, :]).then_inc(wq_in, 16)
            sp.wait_ge(B["added"], 1)
            sp.wait_ge(win_out, 16 * 5)
            sp.dma_start(GAIN, io["gains"][3:4, :].partition_broadcast(P)).then_inc(wq_in, 16)
            sp.dma_start(KEYS, io["keys"][1]).then_inc(wq_in, 16)
            peer_sems[1].wait(sp, "routed", HEADS * TILES)
            sp.dma_start(GAINF, io["gains"][5:6, :].partition_broadcast(P)).then_inc(gainf_in, 16)
            for t in range(TILES):
                n = P if t < FULL else LAST
                sp.wait_ge(y_ready2, t + 1)
                sp.dma_start(io["y"][t * P:t * P + n, :], H[0:n, t, :]).then_inc(y_stored, 16)
            sp.wait_ge(y_stored, 16 * TILES)
            sp.wait_ge(states_out, 32)

        @block.vector
        def _(dve):
            c = Chain(dve, s_dve)

            def mul(out, a, b):
                return dve.tensor_tensor(out, a, b, ALU.mult)

            def times(out_re, out_im, x_re, x_im, y_re, y_im, t1, t2):
                c(mul(t1, x_re, y_re))
                c(mul(t2, x_im, y_im))
                c(dve.tensor_tensor(out_re, t1, t2, ALU.subtract))
                c(mul(t1, x_re, y_im))
                c(mul(t2, x_im, y_re))
                c(dve.tensor_tensor(out_im, t1, t2, ALU.add))

            def exact_exp(out, x):
                k, r, q = w[:, 13, :], w[:, 14, :], w[:, 15, :]
                c(dve.tensor_scalar(x, x, -87.0, 88.0, ALU.max, ALU.min))
                c(dve.tensor_scalar(k, x, 1.4426950408889634, 12582912.0, ALU.mult, ALU.add))
                c(dve.tensor_scalar(k, k, -12582912.0, None, ALU.add))
                c(dve.scalar_tensor_tensor(r, k, -0.693359375, x, ALU.mult, ALU.add))
                c(dve.scalar_tensor_tensor(r, k, 2.12194440e-4, r, ALU.mult, ALU.add))
                c(dve.tensor_scalar(q, r, 1 / 5040, None, ALU.mult))
                for coef in (1 / 720, 1 / 120, 1 / 24, 1 / 6, 1 / 2, 1.0):
                    c(dve.scalar_tensor_tensor(q, q, coef, r, ALU.add, ALU.mult))
                c(dve.tensor_scalar(q, q, 1.0, None, ALU.add))
                c(dve.tensor_scalar(wi[:, :], k, 127.0, 8388608.0, ALU.add, ALU.mult))
                c(mul(out, q, wi[:, :].bitcast(F32)))

            def rsqrt_refined(r, root, v, t):
                c(dve.reciprocal(r, root))
                c(mul(t, r, r))
                c(mul(t, t, v))
                c(dve.tensor_scalar(t, t, -0.5, 1.5, ALU.mult, ALU.add))
                c(mul(r, r, t))

            dve.memset(zero[:, :], 0.0).then_inc(zeroed, 1)
            dve.wait_ge(squares, 1)
            dve.tensor_scalar(st[0:NC, 1, :], st[0:NC, 0, :], 1.0 / D, EPS, ALU.mult, ALU.add).then_inc(roots_in, 1)
            dve.wait_ge(roots, 1)
            rsqrt_refined(st[0:NC, 3, :], st[0:NC, 2, :], st[0:NC, 1, :], st[0:NC, 0, :])
            dve.wait_ge(gain_in, 16)
            for s in range(Q):
                rows = X[0:NC, s, :].rearrange("p (g j) -> p g j", j=GS)
                gain = GAIN0[0:NC, :].rearrange("p (g j) -> p g j", j=GS)
                dve.scalar_tensor_tensor(XN[0:NC, :, s, :], rows, st[0:NC, 3, s:s + 1], gain,
                                         ALU.mult, ALU.mult).then_inc(normed, 1)

            dve.wait_ge(par_in, 16)
            lr, li = par[:, 0, :], par[:, 1, :]
            dt, mag = w[:, 0, :], w[:, 1, :]
            exact_exp(dt, par[:, 2, :])
            c(mul(w[:, 2, :], li, dt))
            c(dve.tensor_scalar(w[:, 3, :], w[:, 2, :], 1 / (2 * PI), 12582912.0, ALU.mult, ALU.add))
            c(dve.tensor_scalar(w[:, 3, :], w[:, 3, :], -12582912.0, None, ALU.add))
            c1 = 6.28125
            c2 = int((2 * PI - c1) * 2 ** 20) / 2 ** 20
            for part in (c1, c2, 2 * PI - c1 - c2):
                c(dve.scalar_tensor_tensor(w[:, 2, :], w[:, 3, :], -part, w[:, 2, :], ALU.mult, ALU.add))
            c(dve.tensor_scalar(w[:, 5, :], w[:, 2, :], 3.1415925, -3.1415925, ALU.min, ALU.max))
            c(dve.scalar_tensor_tensor(w[:, 4, :], w[:, 5, :], -1.0, w[:, 5, :], ALU.mult, ALU.max))
            dve.tensor_scalar(w[:, 4, :], w[:, 4, :], -1.0, PI / 2, ALU.mult, ALU.add).then_inc(angles, 1)
            c(mul(w[:, 8, :], lr, dt))
            exact_exp(mag, w[:, 8, :])
            dve.wait_ge(sines, 1)
            c(mul(pw[:, 0, 1, :], w[:, 6, :], mag))
            c(mul(pw[:, 1, 1, :], w[:, 7, :], mag))
            c(dve.memset(pw[:, 0, 0, :], 1.0))
            c(dve.memset(pw[:, 1, 0, :], 0.0))
            for have in (1, 2, 4):
                x, y = pw[:, :, 1:have + 1, :], pw[:, :, have, :].unsqueeze(2).to_broadcast([P, 2, have, PAIRS])
                t1, t2 = w[:, 8:8 + have, :], w[:, 12:12 + have, :]
                times(pw[:, 0, have + 1:2 * have + 1, :], pw[:, 1, have + 1:2 * have + 1, :],
                      x[:, 0], x[:, 1], y[:, 0], y[:, 1], t1, t2)
            for s in range(Q):
                c(dve.tensor_copy(pwr[:, :, s, :], pw[:, :, Q - 1 - s, :]))
            ar1, t1, t2, fr, fi, rden = (w[:, i, :] for i in range(2, 8))
            c(dve.tensor_scalar(ar1, pw[:, 0, 1, :], -1.0, None, ALU.add))
            c(mul(t1, lr, lr))
            c(mul(t2, li, li))
            c(dve.tensor_tensor(rden, t1, t2, ALU.add))
            c(dve.reciprocal(rden, rden))
            c(mul(t1, ar1, lr))
            c(mul(t2, pw[:, 1, 1, :], li))
            c(dve.tensor_tensor(fr, t1, t2, ALU.add))
            c(mul(fr, fr, rden))
            c(mul(t1, pw[:, 1, 1, :], lr))
            c(mul(t2, ar1, li))
            c(dve.tensor_tensor(fi, t1, t2, ALU.subtract))
            c(mul(fi, fi, rden))
            dve.wait_ge(bc_in, 64)
            bc = [P, PAIRS, GS]
            u1, u2 = (TMP[:, i * 512:(i + 1) * 512].rearrange("p (a b) -> p a b", b=GS) for i in range(2))
            times(Bb[:, 0], Bb[:, 1], BRAW[:, 0], BRAW[:, 1],
                  fr.unsqueeze(2).to_broadcast(bc), fi.unsqueeze(2).to_broadcast(bc), u1, u2)
            dve.wait_ge(turned, NU)
            def powers(t, ri, n):
                return t[:, ri].rearrange("p s q -> p q s").unsqueeze(3).to_broadcast([P, PAIRS, n, GS])

            def over(t, n):
                return t.unsqueeze(2).to_broadcast([P, PAIRS, n, GS])

            tE = TMP[:, 0:PAIRS * BLK].rearrange("p (q s j) -> p q s j", s=Q, j=GS)
            for ri in range(2):
                out = E[:, ri].rearrange("p q (s j) -> p q s j", j=GS)
                c(mul(out, powers(pwr, 0, Q), over(Bb[:, ri], Q)))
                c(mul(tE, powers(pwr, 1, Q), over(Bb[:, 1 - ri], Q)))
                dve.tensor_tensor(E[:, ri].rearrange("p q n -> p (q n)"), E[:, ri].rearrange("p q n -> p (q n)"),
                                  TMP[:, 0:PAIRS * BLK], ALU.add if ri else ALU.subtract).then_inc(e_ready, 1)
                dve.wait_ge(e_ready, ri + 1)
            tC = TMP.rearrange("p (q s j) -> p q s j", s=Q + 1, j=GS)
            for ri in range(2):
                c(mul(CA[:, ri], powers(pw, 0, Q + 1), over(CRAW[:, ri], Q + 1)))
                c(mul(tC, powers(pw, 1, Q + 1), over(CRAW[:, 1 - ri], Q + 1)))
                flat = CA[:, ri].rearrange("p q s j -> p (q s j)")
                if ri == 0:
                    ins = dve.tensor_tensor(flat, flat, TMP, ALU.subtract)
                else:
                    ins = dve.scalar_tensor_tensor(flat, flat, -1.0, TMP, ALU.mult, ALU.subtract)
                ins.then_inc(ca_ready, 1)
                dve.wait_ge(ca_ready, ri + 1)
            for i in range(2):
                for ri in range(2):
                    c(dve.tensor_copy(a8[:, i, ri, :], pw[:, i, Q, :]))
            for ri in range(2):
                c(dve.memset(HP[:, ri, :, 0], 0.0))
                c(dve.tensor_copy(HP[:, ri, :, CH:NC], h0[:, ri].rearrange("p b q -> p q b")))
            dve.wait_ge(turned_out, NU + NW + 2 * PR)
            sk = V[0:GS, :, :, :].rearrange("p a b c -> p (a b c)")[:, 0:G * GS].rearrange("p (g j) -> p g j", j=GS)
            c(mul(sk, ident[0:GS, 0:GS].unsqueeze(1).to_broadcast([GS, G, GS]),
                  dsk[:, :].unsqueeze(2).to_broadcast([GS, G, GS])))
            dve.tensor_tensor(M[0:GS, :, 0:GS], M[0:GS, :, 0:GS], sk, ALU.add).then_inc(skip_added, 1)
            for r, pairs in enumerate(VR):
                dve.wait_ge(v_ready, r + 1)
                for g2 in range(2):
                    v_copy(dve.tensor_copy, r, pairs, 1, g2).then_inc(v_dve, 1)

            dve.wait_ge(v_dve, 2 * len(VR))
            dve.wait_ge(v_act, 2 * len(VR))
            def carry(out, now, v_in, k_ready=None):
                c(mul(pr8[:, :, :, :], a8[:, :, :, :], now.unsqueeze(1).to_broadcast([P, 2, 2, PAIRS])))
                c(dve.tensor_tensor(out, v_in, pr8[:, 0], ALU.add))
                c(dve.tensor_tensor(out[:, 0], out[:, 0], pr8[:, 1, 1], ALU.subtract))
                c(dve.tensor_tensor(out[:, 1], out[:, 1], pr8[:, 1, 0], ALU.add))

            c.reset()
            with dve.Fori(0, CH - 1) as k:
                carry(HP[:, :, :, bass.ds(k + 1, 1)].rearrange("p r q o -> p r (q o)"),
                      HP[:, :, :, bass.ds(k, 1)].rearrange("p r q o -> p r (q o)"),
                      V[:, :, :, bass.ds(k, 1)].rearrange("p r q o -> p r (q o)"))
                c.reset()
            dve.engine_nop().then_inc(scanned, 1)
            carry(hf[:, :, :], HP[:, :, :, CH - 1], V[:, :, :, CH - 1])
            for b in range(NSEQ):
                carry(hs[:, :, b, :], h0[:, :, b, :], V[:, :, :, CH + b])
            dve.engine_nop().then_inc(state_ready, 2)

            for r in range(1, 2 * KT, 2):
                dve.wait_ge(z_ready, r + 1)
                z_copy(dve.tensor_copy, r).then_inc(z_dve, 1)
            dve.wait_ge(y_ready, PR)
            c(dve.memset(H[LAST:P, FULL, :], 0.0))
            dve.wait_ge(h_in, 32)
            for t in range(TILES):
                n = P if t < FULL else LAST
                dve.wait_ge(gate_ready, t + 1)
                gl = ps[0:n, 4 * (t % 2):4 * (t % 2) + 2, :].rearrange("p a b -> p (a b)")
                c(mul(SG[0:n, t % 2, :], SG[0:n, t % 2, :], gl))
                dve.tensor_tensor(H[0:n, t, :], H[0:n, t, :], SG[0:n, t % 2, :], ALU.add).then_inc(mixed, 1)

            def peer(L):
                S = peer_sems[L]

                def mean_square(t):
                    c(dve.scalar_tensor_tensor(XNEXT, H[:, t, :], 1.0, H[:, t, :], ALU.mult, ALU.mult,
                                               accum_out=rt[:, 0:1]))
                    dve.tensor_scalar(rt[:, 0:1], rt[:, 0:1], 1.0 / D, EPS, ALU.mult, ALU.add).then_inc(S["ms_ready"], 1)

                def normalise(t):
                    S.wait(dve, "root_ready", t + 1)
                    rsqrt_refined(rt[:, 2:3], rt[:, 1:2], rt[:, 0:1], rt[:, 3:4])
                    S.wait(dve, "xt_ready", t)
                    dve.scalar_tensor_tensor(XNEXT, H[:, t, :], rt[:, 2:3], GAIN, ALU.mult, ALU.mult)\
                       .then_inc(S["x_ready"], 1)

                def best(par, r, half):
                    if half == 0:
                        S.wait(dve, "sc_copied", r + 1)
                    sc, sc2, v, i = SC[:, par, half, :], SC2[:, half, :], top[:, half, :], topi[:, half, :]
                    c(dve.max(v[:, 0:8], sc))
                    c(dve.max_index(i[:, 0:8], v[:, 0:8], sc))
                    c(dve.match_replace(sc2, v[:, 0:8], sc, LOWEST))
                    c(dve.max(v[:, 8:16], sc2))
                    c(dve.max_index(i[:, 8:16], v[:, 8:16], sc2))

                def merge():
                    c(dve.tensor_tensor(CAND, top[:, 0, :].unsqueeze(2).to_broadcast([P, TOPK, TOPK]),
                                        top[:, 1, :].unsqueeze(1).to_broadcast([P, TOPK, TOPK]), ALU.add))
                    cand, cand2 = (x.rearrange("p a b -> p (a b)") for x in (CAND, CAND2))
                    c(dve.max(best_v[:, 0:8], cand))
                    c(dve.max_index(best_i[:, 0:8], best_v[:, 0:8], cand))
                    c(dve.match_replace(cand2, best_v[:, 0:8], cand, LOWEST))
                    c(dve.max(best_v[:, 8:16], cand2))
                    c(dve.max_index(best_i[:, 8:16], best_v[:, 8:16], cand2))

                def name_experts(r, h):
                    c(dve.tensor_scalar(ab[:, 0, :], best_i[:, :], 4, None, ALU.logical_shift_right))
                    c(dve.tensor_scalar(ab[:, 1, :], best_i[:, :], 15, None, ALU.bitwise_and))
                    full = [P, 2, TOPK, TOPK]
                    c(dve.tensor_tensor(EQ, ab[:, :, :].unsqueeze(3).to_broadcast(full),
                                        iota[:, :].unsqueeze(1).unsqueeze(1).to_broadcast(full), ALU.is_equal))
                    c(mul(EQ, EQ, topi[:, :, :].unsqueeze(2).to_broadcast(full)))
                    c(dve.tensor_reduce(picked[:, :, :], EQ, AX.X, ALU.add))
                    c(dve.scalar_tensor_tensor(EID[:, bass.ds(r * TOPK, TOPK)], picked[:, 0, :], float(NKEY),
                                               picked[:, 1, :], ALU.mult, ALU.add))
                    dve.tensor_copy(FV[:, bass.ds(h, 1), :], best_v[:, :].unsqueeze(1)).then_inc(S["routed"], 1)

                def softmax(t):
                    S.wait(dve, "routed", 8 * t + 8)
                    dve.tensor_tensor(EXPS, FV, FV[:, :, 0:1].to_broadcast([P, HEADS, TOPK]), ALU.subtract)\
                       .then_inc(S["fv_ready"], 1)
                    S.wait(dve, "exp_done", t + 1)
                    c(dve.tensor_reduce(sums[:, 0, :], EXPS, AX.X, ALU.add))
                    c(dve.reciprocal(sums[:, 1, :], sums[:, 0, :]))
                    dve.tensor_tensor(GATE[:, bass.ds(t * P, P)].rearrange("p (h k) -> p h k", k=TOPK), EXPS,
                                      sums[:, 1, :].unsqueeze(2).to_broadcast([P, HEADS, TOPK]), ALU.mult)\
                       .then_inc(S["gated"], 1)
                    S.wait(dve, "gated", t + 1)

                def stage_u(j, par):
                    dve.tensor_copy(idxu[:, par, :], EID[:, bass.ds(j * TOPK, TOPK)]).then_inc(S["idxu_ready"], 1)

                def stage_v(j, par):
                    S.wait(dve, "products", 16 * (j - 1))
                    dve.tensor_copy(idxv[:, par, :], EID[:, bass.ds(j * TOPK, TOPK)]).then_inc(S["idxv_ready"], 1)

                def weigh(j, par):
                    S.wait(dve, "diags", 16 * (j - 1))
                    S.wait(dve, "gelus", j + 1)
                    dve.tensor_tensor(av[:, par, :], ge[:, par, :], GATE[:, bass.ds(j * TOPK, TOPK)], ALU.mult)\
                       .then_inc(S["weights"], 1)

                def dot(j, par, k, n):
                    gate(dve, u_in[k % NU_RING], 16 * (2 * j + k // NU_RING + 1) + L * 16 * 2 * HEADS * TILES)
                    S.wait(dve, "dots", 16 * j + k - 1)
                    dve.tensor_tensor_reduce(JUNK[0:n, k % 2, :], UROWS[0:n, k % NU_RING, :], XCUR[0:n, :], 1.0, 0.0,
                                             ALU.mult, ALU.add, hp[0:n, par, k:k + 1]).then_inc(S["dots"], 1)

                def slot(t, h, par, n, route, first_head, first, last):
                    j = t * 8 + h
                    r = j + 8
                    c.reset()
                    if first_head:
                        S.wait(dve, "x_ready", t + 1)
                        dve.tensor_copy(XCUR, XNEXT).then_inc(S["x_cur"], 1)
                        S.wait(dve, "x_cur", t + 1)
                        if route:
                            mean_square(t + 1)
                    if not last:
                        stage_u(j + 1, 1 - par)
                    for k in range(2):
                        dot(j, par, k, n)
                    if not first:
                        weigh(j - 1, 1 - par)
                    for k in range(2, 6):
                        dot(j, par, k, n)
                    if route and first_head:
                        normalise(t + 1)
                    for k in range(6, 8):
                        dot(j, par, k, n)
                    if route and not first_head:
                        best(par, r, 0)
                    for k in range(8, 10):
                        dot(j, par, k, n)
                    if route and not first_head:
                        best(par, r, 1)
                    for k in range(10, 13):
                        dot(j, par, k, n)
                    if route and not first_head:
                        merge()
                    for k in range(13, 16):
                        dot(j, par, k, n)
                    if route and first_head:
                        best(par, r, 0)
                        best(par, r, 1)
                        merge()
                    if route:
                        name_experts(r, h)
                    stage_v(j, par)

                def tile(t, n, route, first):
                    for par in range(2):
                        slot(t, par, par, n, route, par == 0, first and par == 0, False)
                    if route:
                        with dve.Fori(1, HEADS // 2) as m:
                            for par in range(2):
                                slot(t, 2 * m + par, par, n, route, False, False, False)
                    else:
                        for h in range(2, HEADS):
                            slot(t, h, h % 2, n, route, False, False, h == HEADS - 1)
                    if route:
                        softmax(t + 1)

                dve.wait_ge(wq_in, 64 * (L + 1))
                dve.wait_ge(iota_in, 16)
                mean_square(0)
                normalise(0)
                c.reset()
                with dve.Fori(0, HEADS // 2) as m:
                    for par in range(2):
                        best(par, 2 * m + par, 0)
                        best(par, 2 * m + par, 1)
                        merge()
                        name_experts(2 * m + par, 2 * m + par)
                        c.reset()
                softmax(0)
                stage_u(0, 0)
                tile(0, P, True, True)
                with dve.Fori(1, FULL) as t:
                    tile(t, P, True, False)
                tile(FULL, LAST, False, False)
                weigh(HEADS * TILES - 1, 1)

            def probabilities(S, t, rows, n):
                gate(dve, S["exps"], t + 1)
                c(dve.tensor_tensor(mx[:, 2, 0:n], mx[:, 2, 0:n], mx[:, 3, 0:n], ALU.add))
                c(dve.reciprocal(mx[:, 2, 0:n], mx[:, 2, 0:n]))
                dve.tensor_tensor(rows, rows, mx[:, 2, 0:n].unsqueeze(2).to_broadcast(rows.shape), ALU.mult)\
                   .then_inc(S["probs"], 1)

            def row_max(S, t, rows, n, sink):
                gate(dve, S["masked"], (t + 1) * (QPK if n == QH else NSEQ // 2))
                c(dve.tensor_reduce(mx[:, 0, 0:n], rows, AX.X, ALU.max))
                c(dve.tensor_tensor(mx[:, 0, 0:n], mx[:, 0, 0:n], sink, ALU.max))
                c(dve.tensor_tensor(mx[:, 1, 0:n], sink, mx[:, 0, 0:n], ALU.subtract))
                dve.tensor_scalar(mx[:, 0, 0:n], mx[:, 0, 0:n], -1.0, None, ALU.mult).then_inc(S["max"], 1)

            def att_norm(S, t, tile):
                c(dve.scalar_tensor_tensor(XK, H[:, tile, :], 1.0, H[:, tile, :], ALU.mult, ALU.mult,
                                           accum_out=rt[:, 0:1]))
                dve.tensor_scalar(rt[:, 0:1], rt[:, 0:1], 1.0 / D, EPS, ALU.mult, ALU.add).then_inc(S["ms"], 1)
                gate(dve, S["root"], t + 1)
                rsqrt_refined(rt[:, 2:3], rt[:, 1:2], rt[:, 0:1], rt[:, 3:4])
                for out, gain in ((XK, GKV), (XQ, GMX)):
                    dve.scalar_tensor_tensor(out, H[:, tile, :], rt[:, 2:3], gain, ALU.mult, ALU.mult)\
                       .then_inc(S["x"], 1)

            def add_output(S, t, tile, n):
                gate(dve, S["y"], t + 1)
                flat = H[0:n, bass.ds(tile, 1), :].rearrange("p a d -> p (a d)")
                dve.tensor_tensor(flat, flat, ps[0:n, 4:6, :].rearrange("p a b -> p (a b)"), ALU.add)\
                   .then_inc(S["added"], 1)

            def att_tile(t, mask):
                S = att_sems[0]
                c.reset()
                att_norm(S, t, t)
                gate(dve, S["kt"], t + 1)
                for kvh in range(KVH):
                    rows = slice(kvh * HD, kvh * HD + HD)
                    dve.tensor_copy(KZ[rows, kvh, bass.ds(P + t * P, P)], ps[rows, 3, 0:P]).then_inc(S["kt_copied"], 1)
                for i in range(QPK):
                    gate(dve, S["s"], QPK * t + i + 1)
                    dve.scalar_tensor_tensor(PB[:, i], ps[:, i % 4, :].rearrange("p (a b) -> p a b", a=2), SCALE,
                                             mask.unsqueeze(1).to_broadcast([P, 2, 2 * P]), ALU.mult, ALU.add)\
                       .then_inc(S["masked"], 1)
                rows = PB.rearrange("p a b n -> p (a b) n")
                row_max(S, t, rows, QH, sinks[:, 0:QH])
                probabilities(S, t, rows, QH)
                for r in range(1, QPK, 2):
                    gate(dve, S["pt"], QPK * t + r + 1)
                    pt_copy(dve.tensor_copy, r).then_inc(S["pt_dve"], 1)
                gate(dve, S["o"], t + 1)
                for kvh in range(KVH):
                    rows = slice(kvh * HD, kvh * HD + HD)
                    dve.tensor_copy(OT[rows, :, :].rearrange("p (a i) n -> p a i n", a=4),
                                    ps[rows, 0:4, :].rearrange("p a (i k n) -> p a i k n", i=2, k=2)[:, :, :, kvh, :])\
                       .then_inc(S["o_copied"], 1)
                add_output(S, t, t, P)
                gate(dve, S["added"], t + 1)

            def attention():
                peer_sems[0].wait(dve, "h_done", TILES)
                c(dve.memset(KZ, 0.0))
                c(dve.memset(V2[:, 0, :], 0.0))
                dve.wait_ge(wkv_in, 48)
                dve.wait_ge(wa_in, 64)
                dve.wait_ge(sinks_in, 16)
                att_tile(0, MASK1)
                with dve.Fori(1, FULL) as t:
                    att_tile(t, MASKN)
                S = att_sems[1]
                c.reset()
                att_norm(S, 0, FULL)
                c(dve.memset(QBD, 0.0))
                dve.wait_ge(S["kt"], 1)
                dve.tensor_copy(KNT, ps[:, 3, 0:LAST]).then_inc(S["kt_copied"], 1)
                dve.wait_ge(S["qt"], 1)
                for kvh in range(KVH):
                    rows = slice(kvh * HD, kvh * HD + HD)
                    for half in range(2):
                        out = QBD[rows, :, kvh * HD:kvh * HD + HD].rearrange("p b (i s) -> p i b s", s=STEPS)
                        dve.tensor_copy(out[:, 4 * half:4 * half + 4],
                                        ps[rows, 6 + half, :].rearrange("p (i n) -> p i n", i=4)[:, :, 0:LAST]
                                        .rearrange("p i (b s) -> p i b s", s=STEPS)).then_inc(sample_q, 1)
                for r in range(NSEQ // 2):
                    dve.wait_ge(S["s"], r + 1)
                    dve.scalar_tensor_tensor(SB[:, 2 * r:2 * r + 2, :],
                                             ps[:, r, 0:2 * WIDE].rearrange("p (a b) -> p a b", a=2), SCALE,
                                             SMASK[:, 2 * r:2 * r + 2, :], ALU.mult, ALU.add).then_inc(S["masked"], 1)
                row_max(S, 0, SB, NSEQ, sinks[:, QH:QH + 1].to_broadcast([P, NSEQ]))
                probabilities(S, 0, SB, NSEQ)
                dve.wait_ge(S["o"], 1)
                for kvh in range(KVH):
                    rows = slice(kvh * HD, kvh * HD + HD)
                    for half in range(2):
                        src = ps[rows, 4 + half, :].rearrange("p (b k i s) -> p k i b s", b=4, k=2, s=STEPS)[:, kvh]
                        dst = OT[rows, :, 0:LAST].rearrange("p i (b s) -> p i b s", s=STEPS)
                        dve.tensor_copy(dst[:, :, 4 * half:4 * half + 4], src).then_inc(S["o_copied"], 1)
                add_output(S, 0, FULL, LAST)
                dve.wait_ge(S["added"], 1)

            peer(0)
            attention()
            peer(1)
            dve.wait_ge(gainf_in, 16)
            for t in range(TILES):
                n = P if t < FULL else LAST
                c.reset()
                peer_sems[1].wait(dve, "h_done", t + 1)
                c(dve.scalar_tensor_tensor(YSQ[0:n, :], H[0:n, t, :], 1.0, H[0:n, t, :], ALU.mult, ALU.mult,
                                           accum_out=rt[0:n, 0:1]))
                dve.tensor_scalar(rt[0:n, 0:1], rt[0:n, 0:1], 1.0 / D, EPS, ALU.mult, ALU.add).then_inc(last_ms, 1)
                dve.wait_ge(last_root, t + 1)
                rsqrt_refined(rt[0:n, 2:3], rt[0:n, 1:2], rt[0:n, 0:1], rt[0:n, 3:4])
                dve.scalar_tensor_tensor(H[0:n, t, :], H[0:n, t, :], rt[0:n, 2:3], GAINF[0:n, :], ALU.mult, ALU.mult)\
                   .then_inc(y_ready2, 1)

        @block.scalar
        def _(act):
            c = Chain(act, s_act)
            act.wait_ge(x_in, 16)
            for s in range(Q):
                c(act.activation(SQ[0:NC, :], X[0:NC, s, :], ACT.Square, accum_out=st[0:NC, 0, s:s + 1]))
            act.nop().then_inc(squares, 1)
            act.wait_ge(roots_in, 1)
            act.activation(st[0:NC, 2, :], st[0:NC, 1, :], ACT.Sqrt).then_inc(roots, 1)

            def turned_copy(r, out, src):
                act.wait_ge(turned, r + 1)
                act.copy(out, src).then_inc(turned_out, 1)

            for r, groups in enumerate(UR):
                n = len(groups)
                turned_copy(r, U[:, groups[0]:groups[0] + n, :].rearrange("p g n -> p (g n)"), ps[:, r % 4, 0:n * NC])
            act.wait_ge(angles, 1)
            act.activation(w[:, 6:8, :], w[:, 4:6, :], ACT.Sin).then_inc(sines, 1)
            for r, (ri, q0) in enumerate(WR):
                turned_copy(NU + r, WIN[:, q0:q0 + 4, :, ri, :],
                            ps[:, (NU + r) % 4, :].rearrange("p (q g n) -> p q g n", q=4, g=2))
            for r in range(PR):
                act.wait_ge(turned, NU + NW + r + 1)
                for g2 in range(2):
                    act.copy(M[0:GS, 8 * r + g2:8 * r + 8:2, :],
                             ps[0:GS, 4 + 2 * (r % 2) + g2, :].rearrange("p (q n) -> p q n", q=4)).then_inc(turned_out, 1)
            act.wait_ge(ca_ready, 2)
            act.wait_ge(skip_added, 1)
            for r, pairs in enumerate(VR):
                act.wait_ge(v_ready, r + 1)
                for g2 in range(2):
                    v_copy(act.copy, r, pairs, 0, g2).then_inc(v_act, 1)
            act.wait_ge(m_out, 16)
            for r in range(PR):
                act.wait_ge(y_ready, r + 1)
                for g2 in range(2):
                    z = Z[0:NC, :, 8 * GS * r:8 * GS * (r + 1)].rearrange("p t (q g j) -> p g q t j", g=2, j=GS)
                    act.activation(z[:, g2], ps[0:NC, 2 * (r % 4) + g2, :].rearrange("p (q t j) -> p q t j", q=4, j=GS),
                                   ACT.Gelu).then_inc(y_out, 1)
            for r in range(0, 2 * KT, 2):
                act.wait_ge(z_ready, r + 1)
                z_copy(act.copy, r).then_inc(z_act, 1)
            for t in range(TILES):
                n = P if t < FULL else LAST
                act.wait_ge(glu_ready, t + 1)
                if t >= 2:
                    act.wait_ge(mixed, t - 1)
                act.activation(SG[0:n, t % 2, :],
                               ps[0:n, 4 * (t % 2) + 2:4 * (t % 2) + 4, :].rearrange("p a b -> p (a b)"),
                               ACT.Sigmoid).then_inc(gate_ready, 1)

            def peer(L):
                S = peer_sems[L]

                def root(t):
                    S.wait(act, "ms_ready", t + 1)
                    act.activation(rt[:, 1:2], rt[:, 0:1], ACT.Sqrt).then_inc(S["root_ready"], 1)

                def xt_copy(t):
                    S.wait(act, "q_ready", 8 * t)
                    for i in range(2):
                        S.wait(act, "xt_ready", t + 1)
                        act.copy(XT[:, 4 * i:4 * i + 4, :].rearrange("p k n -> p (k n)"), ps[:, 2 + i, :])\
                           .then_inc(S["xt_copied"], 1)

                def q_copy(r, par):
                    S.wait(act, "q_ready", r + 1)
                    S.wait(act, "qt_ready", r - 1)
                    act.copy(QN[:, par, :], ps[:, 4 + par, 0:2 * P]).then_inc(S["q_copied"], 1)

                def qt_copy(r, par):
                    S.wait(act, "qt_ready", r + 1)
                    S.wait(act, "sc_ready", r - 1)
                    act.copy(QT[:, par].rearrange("p a n -> p (a n)"), ps[:, 6 + par, 0:2 * P]).then_inc(S["qt_copied"], 1)

                def sc_copy(r, par):
                    S.wait(act, "sc_ready", r + 1)
                    S.wait(act, "routed", r - 1)
                    act.copy(SC[:, par].rearrange("p a n -> p (a n)"), ps[:, 6 + par, 256:512]).then_inc(S["sc_copied"], 1)

                def exps(t):
                    S.wait(act, "fv_ready", t + 1)
                    flat = EXPS.rearrange("p h k -> p (h k)")
                    act.activation(flat, flat, ACT.Exp).then_inc(S["exp_done"], 1)

                def gelu(j, par, n):
                    S.wait(act, "dots", 16 * j + 16)
                    S.wait(act, "weights", j - 1)
                    act.activation(ge[0:n, par, :], hp[0:n, par, :], ACT.Gelu).then_inc(S["gelus"], 1)

                def diag(j, par, k, n):
                    if k == 0:
                        S.wait(act, "weights", j + 1)
                    S.wait(act, "products", 16 * j + k - 3)
                    act.activation(DIAG[0:n, k % 4, 0:n], ident[0:n, 0:n], ACT.Copy, scale=av[0:n, par, k:k + 1])\
                       .then_inc(S["diags"], 1)

                def store(t, n):
                    S.wait(act, "products", 128 * t + 128)
                    act.copy(H[0:n, bass.ds(t, 1), :].rearrange("p a d -> p (a d)"),
                             ps[0:n, 0:2, :].rearrange("p a b -> p (a b)")).then_inc(S["h_done"], 1)

                def slot(t, h, par, n, route, first_head, first):
                    j, r, m = t * 8 + h, t * 8 + h + 8, 1 - par
                    nv = P if first_head else n
                    if route and first_head:
                        root(t + 1)
                    if not first:
                        gelu(j - 1, m, nv)
                    if route and not first_head:
                        q_copy(r, par)
                    if not first:
                        for k in range(0, 4):
                            diag(j - 1, m, k, nv)
                    if route and first_head:
                        xt_copy(t + 1)
                    if route and not first_head:
                        qt_copy(r, par)
                    if not first:
                        for k in range(4, 8):
                            diag(j - 1, m, k, nv)
                    if route and first_head:
                        q_copy(r, par)
                    if route and not first_head:
                        sc_copy(r, par)
                    if not first:
                        for k in range(8, 12):
                            diag(j - 1, m, k, nv)
                    if route and first_head:
                        qt_copy(r, par)
                    if not first:
                        for k in range(12, 16):
                            diag(j - 1, m, k, nv)
                    if route and first_head:
                        sc_copy(r, par)
                    if first_head and not first:
                        store(t - 1, P)

                def tile(t, n, route, first):
                    for par in range(2):
                        slot(t, par, par, n, route, par == 0, first and par == 0)
                    with act.Fori(1, HEADS // 2) as m:
                        for par in range(2):
                            slot(t, 2 * m + par, par, n, route, False, False)
                    if route:
                        exps(t + 1)

                root(0)
                xt_copy(0)
                def copies(m):
                    for par in range(2):
                        q_copy(2 * m + par, par)
                        qt_copy(2 * m + par, par)
                        sc_copy(2 * m + par, par)

                copies(0)
                with act.Fori(1, HEADS // 2) as m:
                    copies(m)
                exps(0)
                tile(0, P, True, True)
                with act.Fori(1, FULL) as t:
                    tile(t, P, True, False)
                tile(FULL, LAST, False, False)
                j = HEADS * TILES - 1
                gelu(j, 1, LAST)
                for k in range(16):
                    diag(j, 1, k, LAST)
                store(FULL, LAST)

            def root_of(S, t):
                gate(act, S["ms"], t + 1)
                act.activation(rt[:, 1:2], rt[:, 0:1], ACT.Sqrt).then_inc(S["root"], 1)

            def att_project(S, t):
                root_of(S, t)
                for which, out in enumerate((XKT, XQT)):
                    gate(act, S["xt"], 2 * t + which + 1)
                    for i in range(2):
                        act.copy(out[:, 4 * i:4 * i + 4, :].rearrange("p k n -> p (k n)"), ps[:, i, :])\
                           .then_inc(S["xt_copied"], 1)
                    if which == 0:
                        gate(act, S["kv"], t + 1)
                        act.copy(KVN, ps[:, 2, 0:2 * P]).then_inc(S["kv_copied"], 1)
                        act.copy(V2[:, 1, :], ps[:, 2, P:2 * P]).then_inc(S["kv_copied"], 1)
                gate(act, S["q"], t + 1)
                act.copy(QNA, ps[:, 4:6, :].rearrange("p a b -> p (a b)")).then_inc(S["q_copied"], 1)

            def att_exps(S, t, rows, n):
                gate(act, S["max"], t + 1)
                act.activation(mx[:, 3, 0:n], mx[:, 1, 0:n], ACT.Exp)
                for i in range(n):
                    last = act.activation(rows[:, i, :], rows[:, i, :], ACT.Exp, bias=mx[:, 0, i:i + 1],
                                          accum_out=mx[:, 2, i:i + 1])
                last.then_inc(S["exps"], 1)

            def att_tile(t):
                S = att_sems[0]
                att_project(S, t)
                gate(act, S["qt"], t + 1)
                act.copy(QTA.rearrange("p i n -> p (i n)"), ps[:, 6:8, :].rearrange("p a b -> p (a b)"))\
                   .then_inc(S["qt_copied"], 1)
                att_exps(S, t, PB.rearrange("p a b n -> p (a b) n"), QH)
                for r in range(0, QPK, 2):
                    gate(act, S["pt"], QPK * t + r + 1)
                    pt_copy(act.copy, r).then_inc(S["pt_act"], 1)
                gate(act, S["o"], t + 1)
                act.copy(V2[:, 0, :], V2[:, 1, :]).then_inc(S["pt_act"], 1)
                gate(act, S["pt_act"], 5 * (t + 1))

            def attention():
                att_tile(0)
                with act.Fori(1, FULL) as t:
                    att_tile(t)
                S = att_sems[1]
                act.wait_ge(win_out, 48)
                att_project(S, 0)
                act.wait_ge(S["pt"], 1)
                act.copy(KBT.rearrange("p b n -> p (b n)"), ps[:, 0:2, :].rearrange("p a b -> p (a b)"))\
                   .then_inc(S["pt_act"], 1)
                att_exps(S, 0, SB, NSEQ)
                act.wait_ge(S["pt"], 2)
                act.copy(PTB.rearrange("p b n -> p (b n)"), ps[:, 4:6, :].rearrange("p a b -> p (a b)"))\
                   .then_inc(S["pt_act"], 1)
                act.wait_ge(S["pt"], 3)
                act.copy(PTN[0:LAST].rearrange("p b n -> p (b n)"), ps[0:LAST, 6:8, :].rearrange("p a b -> p (a b)"))\
                   .then_inc(S["pt_act"], 1)

            peer(0)
            attention()
            peer(1)
            for t in range(TILES):
                n = P if t < FULL else LAST
                act.wait_ge(last_ms, t + 1)
                act.activation(rt[0:n, 1:2], rt[0:n, 0:1], ACT.Sqrt).then_inc(last_root, 1)

        @block.tensor
        def _(pe):
            pe.wait_ge(ident_in, 16)
            pe.wait_ge(normed, Q)
            for r, groups in enumerate(UR):
                if r >= 4:
                    pe.wait_ge(turned_out, r - 3)
                for i, g in enumerate(groups):
                    mm = pe.transpose(ps[:, r % 4, i * NC:(i + 1) * NC], XN[0:NC, g, :, :].rearrange("p s j -> p (s j)"), ident[0:NC, 0:NC])
                mm.then_inc(turned, 1)
            for r, (ri, q0) in enumerate(WR):
                n = NU + r
                pe.wait_ge(e_ready, ri + 1)
                pe.wait_ge(turned_out, n - 3)
                for i in range(4):
                    mm = pe.transpose(ps[:, n % 4, i * P:(i + 1) * P], E[:, ri, q0 + i, :], ident[:, :])
                mm.then_inc(turned, 1)
            pe.wait_ge(ca_ready, 2)
            for r in range(PR):
                if r >= 2:
                    pe.wait_ge(turned_out, NU + NW + 2 * (r - 1))
                for i in range(8):
                    q, g2 = 4 * r + i // 2, i % 2
                    rows = slice(SD * g2, SD * g2 + SD)
                    out = ps[0:GS, 4 + 2 * (r % 2) + g2, (i // 2) * BLK:(i // 2 + 1) * BLK]
                    for ri in range(2):
                        mm = pe.matmul(out, Bb[rows, ri, q, :],
                                       CA[rows, ri, q, 0:Q, :].rearrange("p s j -> p (s j)"),
                                       start=(ri == 0), stop=(ri == 1))
                mm.then_inc(turned, 1)
            pe.wait_ge(turned_out, NU + NW + 2 * PR)
            for r, pairs in enumerate(VR):
                if r >= 4:
                    pe.wait_ge(v_act, 2 * (r - 3))
                    pe.wait_ge(v_dve, 2 * (r - 3))
                half = len(pairs) // 2
                for i, q in enumerate(pairs):
                    for g2 in range(2):
                        b, j = 2 * (r % 4) + i // half, 2 * (i % half) + g2
                        mm = pe.matmul(ps[:, b, j * NC:(j + 1) * NC],
                                       WIN[:, q, g2, :, :].rearrange("p r n -> p (r n)"), U[:, 2 * q + g2, :],
                                       start=True, stop=True)
                mm.then_inc(v_ready, 1)
            pe.wait_ge(k_in, 16 * Q)
            pe.wait_ge(scanned, 1)
            pe.wait_ge(v_act, 2 * len(VR))
            for r in range(PR):
                if r >= 4:
                    pe.wait_ge(y_out, 2 * (r - 3))
                for i in range(8):
                    g, q, g2 = 8 * r + i, 4 * r + i // 2, i % 2
                    rows = slice(SD * g2, SD * g2 + SD)
                    out = ps[0:NC, 2 * (r % 4) + g2, (i // 2) * BLK:(i // 2 + 1) * BLK]
                    pe.matmul(out, U[:, g, :], K[:, g, :], start=True, stop=False)
                    for ri in range(2):
                        mm = pe.matmul(out, HP[rows, ri, q, :],
                                       CA[rows, ri, q, 1:Q + 1, :].rearrange("p s j -> p (s j)"),
                                       start=False, stop=(ri == 1))
                mm.then_inc(y_ready, 1)
            pe.wait_ge(y_out, 2 * PR)
            for r in range(2 * KT):
                kt, half = r // 2, r % 2
                if r >= 4:
                    pe.wait_ge(z_act if r % 2 == 0 else z_dve, (r - 4) // 2 + 1)
                for i in range(4):
                    mm = pe.transpose(ps[:, r % 4, i * NC:(i + 1) * NC],
                                      Z[0:NC, 4 * half + i, kt * P:(kt + 1) * P], ident[0:NC, 0:NC])
                mm.then_inc(z_ready, 1)
            pe.wait_ge(z_act, KT)
            pe.wait_ge(z_dve, KT)
            pe.wait_ge(glu_in, 32)
            for t in range(TILES):
                n = P if t < FULL else LAST
                if t >= 2:
                    pe.wait_ge(mixed, t - 1)
                for b in range(4):
                    for kt in range(KT):
                        mm = pe.matmul(ps[0:n, 4 * (t % 2) + b, :], ZT[:, kt, t * P:t * P + n],
                                       WGLU[:, kt, 512 * b:512 * (b + 1)], start=(kt == 0), stop=(kt == KT - 1))
                mm.then_inc(glu_ready, 1)

            def peer(L):
                S = peer_sems[L]

                def xt(t):
                    S.wait(pe, "x_ready", t + 1)
                    S.wait(pe, "xt_copied", 2 * t)
                    for k in range(KT):
                        mm = pe.transpose(ps[:, 2 + k // 4, (k % 4) * P:(k % 4 + 1) * P], XNEXT[:, k * P:(k + 1) * P],
                                          ident[:, :])
                    mm.then_inc(S["xt_ready"], 1)

                def queries(t, h, par):
                    r = 8 * t + h
                    S.wait(pe, "xt_copied", 2 * t + 2)
                    S.wait(pe, "q_copied", r - 1)
                    for k in range(KT):
                        mm = pe.matmul(ps[:, 4 + par, 0:2 * P], XT[:, k, :],
                                       WQ[k // 4][:, k % 4, bass.ds(h * 2 * P, 2 * P)], start=(k == 0), stop=(k == KT - 1))
                    mm.then_inc(S["q_ready"], 1)

                def turn_queries(r, par):
                    S.wait(pe, "q_copied", r + 1)
                    S.wait(pe, "sc_copied", r - 1)
                    for i in range(2):
                        mm = pe.transpose(ps[:, 6 + par, i * P:(i + 1) * P], QN[:, par, i * P:(i + 1) * P], ident[:, :])
                    mm.then_inc(S["qt_ready"], 1)

                def scores(r, h, par):
                    S.wait(pe, "qt_copied", r + 1)
                    for i in range(2):
                        mm = pe.matmul(ps[:, 6 + par, 256 + i * P:256 + (i + 1) * P], QT[:, par, i, :],
                                       KEYS[:, bass.ds(2 * h + i, 1), :].rearrange("p a n -> p (a n)"),
                                       start=True, stop=True)
                    mm.then_inc(S["sc_ready"], 1)

                def start(t, n):
                    S.wait(pe, "h_done", t)
                    for i in range(2):
                        pe.matmul(ps[0:n, i, :], ident[0:n, 0:n],
                                  H[0:n, bass.ds(t, 1), i * 512:(i + 1) * 512].rearrange("p a d -> p (a d)"),
                                  start=True, stop=False, skip_group_check=True)

                def product(j, k, n):
                    S.wait(pe, "diags", 16 * j + k + 1)
                    gate(pe, v_in[k % NV_RING], 16 * (4 * j + k // NV_RING + 1) + L * 16 * 4 * HEADS * TILES)
                    for i in range(2):
                        mm = pe.matmul(ps[0:n, i, :], DIAG[0:n, k % 4, 0:n],
                                       VROWS[0:n, k % NV_RING, i * 512:(i + 1) * 512],
                                       start=False, stop=False, skip_group_check=True)
                    mm.then_inc(S["products"], 1)

                def slot(t, h, par, n, route, first_head, first):
                    j, r = t * 8 + h, t * 8 + h + 8
                    nv = P if first_head else n
                    if route and not first_head:
                        queries(t + 1, h, par)
                    if not first:
                        for k in range(0, 4):
                            product(j - 1, k, nv)
                    if route and first_head:
                        xt(t + 1)
                    if route and not first_head:
                        turn_queries(r, par)
                    if not first:
                        for k in range(4, 8):
                            product(j - 1, k, nv)
                    if route and first_head:
                        queries(t + 1, h, par)
                    if route and not first_head:
                        scores(r, h, par)
                    if not first:
                        for k in range(8, 12):
                            product(j - 1, k, nv)
                    if route and first_head:
                        turn_queries(r, par)
                    if not first:
                        for k in range(12, 16):
                            product(j - 1, k, nv)
                    if route and first_head:
                        scores(r, h, par)
                    if first_head:
                        start(t, n)

                def tile(t, n, route, first):
                    for par in range(2):
                        slot(t, par, par, n, route, par == 0, first and par == 0)
                    with pe.Fori(1, HEADS // 2) as m:
                        for par in range(2):
                            slot(t, 2 * m + par, par, n, route, False, False)

                pe.wait_ge(mixed, TILES)
                pe.wait_ge(wq_in, 64 * (L + 1))
                xt(0)
                def route_pair(m):
                    for par in range(2):
                        queries(0, 2 * m + par, par)
                        turn_queries(2 * m + par, par)
                        scores(2 * m + par, 2 * m + par, par)

                route_pair(0)
                with pe.Fori(1, HEADS // 2) as m:
                    route_pair(m)
                tile(0, P, True, True)
                with pe.Fori(1, FULL) as t:
                    tile(t, P, True, False)
                tile(FULL, LAST, False, False)
                for k in range(16):
                    product(HEADS * TILES - 1, k, LAST)

            def att_project(S, t):
                for which, (x, xt, out, w) in enumerate(((XK, XKT, ps[:, 2:3, 0:2 * P], WKV), (XQ, XQT, ps[:, 4:6, :], WQA))):
                    gate(pe, S["x"], 2 * t + which + 1)
                    if which == 1:
                        gate(pe, S["xt_copied"], 4 * t + 2)
                    for k in range(KT):
                        mm = pe.transpose(ps[:, k // 4, (k % 4) * P:(k % 4 + 1) * P], x[:, k * P:(k + 1) * P], ident[:, :])
                    mm.then_inc(S["xt"], 1)
                    gate(pe, S["xt_copied"], 4 * t + 2 * which + 2)
                    n = out.shape[2]
                    for b in range(out.shape[1]):
                        for k in range(KT):
                            mm = pe.matmul(out[:, b, :], xt[:, k, :], w[:, k, b * n:(b + 1) * n],
                                           start=(k == 0), stop=(k == KT - 1))
                    mm.then_inc(S["q"] if which else S["kv"], 1)
                    if which == 0:
                        gate(pe, S["kv_copied"], 2 * t + 2)
                        pe.transpose(ps[:, 3, 0:P], KVN[:, 0:P], ident[:, :]).then_inc(S["kt"], 1)
                gate(pe, S["q_copied"], t + 1)
                for i in range(QPK):
                    mm = pe.transpose(ps[:, 6 + i // 4, (i % 4) * P:(i % 4 + 1) * P], QNA[:, i * P:(i + 1) * P], ident[:, :])
                mm.then_inc(S["qt"], 1)

            def att_output(S, t, n, copied):
                gate(pe, S["o_copied"], copied)
                for b in range(2):
                    for i in range(QPK):
                        mm = pe.matmul(ps[0:n, 4 + b, :], OT[:, i, 0:n], WO[:, i, b * 512:(b + 1) * 512],
                                       start=(i == 0), stop=(i == QPK - 1))
                mm.then_inc(S["y"], 1)

            def att_tile(t):
                S = att_sems[0]
                gate(pe, S["added"], t)
                att_project(S, t)
                gate(pe, S["qt_copied"], t + 1)
                gate(pe, S["kt_copied"], 2 * t + 2)
                for i in range(QPK):
                    if i >= 4:
                        gate(pe, S["masked"], QPK * t + i - 3)
                    pe.matmul(ps[:, i % 4, :], QTA[:, i, :], KZ[:, :, bass.ds(t * P, 2 * P)],
                              start=True, stop=True).then_inc(S["s"], 1)
                gate(pe, S["probs"], t + 1)
                for r in range(QPK):
                    for half in range(2):
                        for kvh in range(KVH):
                            at = (2 * half + kvh) * P
                            mm = pe.transpose(ps[:, r, at:at + P], PB[:, r, kvh, half * P:(half + 1) * P], ident[:, :])
                    mm.then_inc(S["pt"], 1)
                gate(pe, S["pt_act"], 5 * t + 4)
                gate(pe, S["pt_dve"], 4 * t + 4)
                for r in range(QPK // 2):
                    for half in range(2):
                        mm = pe.matmul(ps[:, r, :], V2[:, half, :],
                                       PT[:, half, 2 * r:2 * r + 2].rearrange("p i k n -> p (i k n)"),
                                       start=(half == 0), stop=(half == 1))
                mm.then_inc(S["o"], 1)
                att_output(S, t, P, 2 * t + 2)

            def attention():
                att_tile(0)
                with pe.Fori(1, FULL) as t:
                    att_tile(t)
                S = att_sems[1]
                pe.wait_ge(att_sems[0]["added"], FULL)
                att_project(S, 0)
                pe.wait_ge(buf_in, 32)
                for b in range(NSEQ):
                    mm = pe.transpose(ps[:, b // 4, (b % 4) * P:(b % 4 + 1) * P], KBUF[:, b, :], ident[:, :])
                mm.then_inc(S["pt"], 1)
                pe.wait_ge(S["pt_act"], 1)
                pe.wait_ge(S["kt_copied"], 1)
                pe.wait_ge(sample_q, 4)
                for r in range(NSEQ // 2):
                    for b in range(2):
                        q = QBD[:, 2 * r + b, :]
                        pe.matmul(ps[:, r, b * WIDE:b * WIDE + P], q, KBT[:, 2 * r + b, :], start=True, stop=True)
                        mm = pe.matmul(ps[:, r, b * WIDE + P:(b + 1) * WIDE], q, KNT, start=True, stop=True)
                    mm.then_inc(S["s"], 1)
                pe.wait_ge(S["probs"], 1)
                for b in range(NSEQ):
                    mm = pe.transpose(ps[:, 4 + b // 4, (b % 4) * P:(b % 4 + 1) * P], SB[:, b, 0:P], ident[:, :])
                mm.then_inc(S["pt"], 1)
                for b in range(NSEQ):
                    mm = pe.transpose(ps[0:LAST, 6 + b // 4, (b % 4) * P:(b % 4 + 1) * P], SB[:, b, P:WIDE], ident[:, :])
                mm.then_inc(S["pt"], 1)
                pe.wait_ge(S["pt_act"], 3)
                for b in range(NSEQ):
                    out = ps[:, 4 + b // 4, (b % 4) * P:(b % 4 + 1) * P]
                    pe.matmul(out, VBUF[:, b, :], PTB[:, b, :], start=True, stop=False)
                    mm = pe.matmul(out, V2[0:LAST, 1, :], PTN[0:LAST, b, :], start=False, stop=True)
                mm.then_inc(S["o"], 1)
                att_output(S, 0, LAST, 4)
                pe.wait_ge(S["added"], 1)

            peer(0)
            attention()
            peer(1)

        @block.gpsimd
        def _(pool):
            def peer(L):
                S = peer_sems[L]
                tab_u, tab_v = io[f"peer_u{L}"], io[f"peer_v{L}"]

                def gather_u(j, par, k, n):
                    S.wait(pool, "dots", 16 * j + k + 1 - NU_RING)
                    pool.indirect_dma_start(UROWS[0:n, k % NU_RING, :], None, tab_u,
                                            bass.IndirectOffsetOnAxis(ap=idxu[0:n, par, k:k + 1], axis=0))\
                        .then_inc(u_in[k % NU_RING], 16)

                def gather_v(j, par, k, n):
                    S.wait(pool, "products", 16 * j + k + 1 - NV_RING)
                    pool.indirect_dma_start(VROWS[0:n, k % NV_RING, :], None, tab_v,
                                            bass.IndirectOffsetOnAxis(ap=idxv[0:n, par, k:k + 1], axis=0))\
                        .then_inc(v_in[k % NV_RING], 16)

                def slot(t, h, par, n, first_head, first):
                    j = t * 8 + h
                    S.wait(pool, "idxu_ready", j + 1)
                    if not first:
                        S.wait(pool, "idxv_ready", j)
                    for k in range(TOPK):
                        gather_u(j, par, k, n)
                        if not first:
                            gather_v(j - 1, 1 - par, k, P if first_head else n)

                def tile(t, n, first):
                    for par in range(2):
                        slot(t, par, par, n, par == 0, first and par == 0)
                    with pool.Fori(1, HEADS // 2) as m:
                        for par in range(2):
                            slot(t, 2 * m + par, par, n, False, False)

                tile(0, P, True)
                with pool.Fori(1, FULL) as t:
                    tile(t, P, False)
                tile(FULL, LAST, False)
                j = HEADS * TILES - 1
                S.wait(pool, "idxv_ready", j + 1)
                for k in range(TOPK):
                    gather_v(j, 1, k, LAST)

            peer(0)
            pool.wait_ge(att_sems[1]["added"], 1)
            peer(1)


def _laid_out(inp):
    import numpy as np

    def states(a):
        a = np.moveaxis(a.reshape(*a.shape[:-2], PAIRS, 2, SD), (-2, -1), (0, 1))
        return a.reshape(P, *a.shape[2:])

    f = {k: np.asarray(v) for k, v in inp.items()}
    x = np.concatenate([f["x_prompt"].reshape(SEQ, D), f["x_sample"].reshape(TOK - SEQ, D)])
    lam = [f["ssm_lam_re"][0], f["ssm_lam_im"][0], np.broadcast_to(f["ssm_log_dt"][0][:, None], (G, SD))]
    row, col = np.arange(P)[:, None], np.arange(2 * P)[None, :]
    seen = (row + P - col >= 0) & (row + P - col < P)
    masks = np.concatenate([np.where(seen & (col >= P), 0.0, NEG), np.where(seen, 0.0, NEG)], 1).astype(np.float32)
    step, b, col = (row % STEPS)[:, :, None], np.arange(NSEQ)[None, :, None], np.arange(WIDE)[None, None, :]
    new = col - P
    seen = np.where(new < 0, step + P - col < P, (new // STEPS == b) & (new % STEPS <= step))
    smask = np.where(seen, 0.0, NEG).astype(np.float32)
    out = {
        "x": x,
        "ident": np.eye(P, dtype=np.float32),
        "gains": np.concatenate([f["norm_mix"], f["norm_ffn"], f["norm_kv"][None], f["norm_final"][None]]),
        "s5par": np.stack([states(a) for a in lam], 1),
        "s5b": np.stack([states(f[n][0].transpose(2, 0, 1)).transpose(0, 2, 1) for n in ("ssm_b_re", "ssm_b_im")], 1),
        "s5c": np.stack([states(f[n][0].transpose(1, 0, 2)).transpose(0, 2, 1) for n in ("ssm_c_re", "ssm_c_im")], 1),
        "h0": np.stack([states(f[n][0]) for n in ("state_ssm_re", "state_ssm_im")], 1),
        "dskip": f["ssm_d"][0].reshape(G, GS).T,
        "w_glu": f["ssm_w_glu"][0],
        "iota": np.broadcast_to(np.arange(TOPK, dtype=np.float32), (P, TOPK)),
        "peer_wq": f["peer_w_q"],
        "w_q": f["w_q"][0].reshape(D, KVH, QPK, HD).transpose(0, 2, 1, 3).reshape(D, D),
        "w_o": f["w_o"][0].reshape(KVH, QPK, HD, D).transpose(1, 0, 2, 3).reshape(D, D),
        "w_kv": f["w_kv"],
        "k_buf": f["cache_k_win"].reshape(NSEQ, P, KVH * HD),
        "v_buf": f["cache_v_win"].reshape(NSEQ, P, KVH * HD),
        "masks": masks, "smask": smask,
        "sinks": np.concatenate([np.broadcast_to(f["attn_sinks"][0].reshape(KVH, QPK).T.reshape(1, QH), (P, QH)),
                                 np.repeat(f["attn_sinks"][0], STEPS)[:, None]], 1),
        "keys": f["peer_sub_keys"].transpose(0, 4, 1, 2, 3).reshape(2, P, 2 * HEADS, NKEY),
        "peer_u0": f["peer_u"][0], "peer_u1": f["peer_u"][1],
        "peer_v0": f["peer_v"][0], "peer_v1": f["peer_v"][1],
    }
    return {k: np.ascontiguousarray(v) for k, v in out.items()}


_OUTS = {"hs": (P, 2, NSEQ, PAIRS), "hf": (P, 2, PAIRS), "y": (TOK, D), "kv_p": (P, 2 * P), "kv_s": (2, NSEQ, P, P)}
_SCRATCH = {"kern": (G, GS, (2 * Q - 1) * GS)}


def kernel(**inputs):
    import numpy as np
    import concourse.bacc as bacc
    from concourse.bass_utils import run_bass_kernel_spmd

    nc = bacc.Bacc("TRN2", target_bir_lowering=False, num_devices=1)
    arrays = {f"in_{k}": v for k, v in _laid_out(inputs).items()}
    io = {k[3:]: nc.dram_tensor(k, v.shape, mybir.dt.from_np(v.dtype), kind="ExternalInput").ap()
          for k, v in arrays.items()}
    for k, shape in _OUTS.items():
        io[k] = nc.dram_tensor(f"out_{k}", shape, F32, kind="ExternalOutput").ap()
    for k, shape in _SCRATCH.items():
        io[k] = nc.dram_tensor(k, shape, F32, kind="Internal").ap()
    build(nc, io)
    got = run_bass_kernel_spmd(nc, [arrays], core_ids=[0]).results[0]

    def groups(a):
        a = np.moveaxis(a.reshape(2, SD, *a.shape[1:]), (0, 1), (-2, -1))
        return a.reshape(*a.shape[:-3], G, SD)

    hs, hf, y, kvp, kvs = (got[f"out_{k}"] for k in ("hs", "hf", "y", "kv_p", "kv_s"))
    return (y[:SEQ].reshape(1, SEQ, D), y[SEQ:].reshape(NSEQ, STEPS, D),
            groups(hf[:, 0])[None, None], groups(hf[:, 1])[None, None],
            kvp[:, :P].reshape(1, P, KVH, HD), kvp[:, P:].reshape(1, P, KVH, HD),
            groups(hs[:, 0])[None], groups(hs[:, 1])[None],
            kvs[0].reshape(NSEQ, P, KVH, HD), kvs[1].reshape(NSEQ, P, KVH, HD))
```

```python
from contextlib import ExitStack

import concourse.bass as bass
from concourse import mybir

ALU = mybir.AluOpType
ACT = mybir.ActivationFunctionType
AX = mybir.AxisListType
F32 = mybir.dt.float32
BF16 = mybir.dt.bfloat16
I32 = mybir.dt.int32
U32 = mybir.dt.uint32

P = 128
D = 1024
KT = D // P
SEQ, NSEQ, STEPS = 512, 8, 8
TOK = SEQ + NSEQ * STEPS
FULL = SEQ // P
TILES = FULL + 1
LAST = TOK - SEQ
Q = 8
CH = SEQ // Q
NC = CH + NSEQ
G, GS, SD = 64, 16, 64
PAIRS = G // 2
BLK = Q * GS
HEADS, NKEY, TOPK = 8, 128, 16
QH, KVH, HD = 16, 2, 64
QPK = QH // KVH
WIDE = P + LAST
SCALE = HD ** -0.5
EPS = 1e-5
NEG = -1.0e30
LOWEST = -3.0e38
PI = 3.141592653589793


class Chain:

    def __init__(self, eng, sem):
        self.eng, self.sem, self.n = eng, sem, 0

    def __call__(self, ins):
        ins.then_inc(self.sem, 1)
        self.n += 1
        self.eng.wait_ge(self.sem, self.n)

    def reset(self):
        self.eng.sem_clear(self.sem)
        self.n = 0


NU_RING, NV_RING = 8, 8
SLOTS = HEADS * FULL + HEADS // 2
PACKED = HEADS * FULL
PE_ROWS = [k for k in range(TOPK) if k % 4 != 3]
DVE_ROWS = [k for k in range(TOPK) if k % 4 == 3]


def pe_rows(j):
    return list(range(TOPK)) if isinstance(j, int) and j >= PACKED else PE_ROWS


def products_before(j):
    n = len(PE_ROWS)
    return n * PACKED + TOPK * (j - PACKED) if isinstance(j, int) and j > PACKED else n * j


def gate(eng, sem, value):
    if isinstance(value, int):
        if value > 0:
            eng.wait_ge(sem, value)
    else:
        eng.wait_ge(sem, value)
        eng.nop(nofuse=True)


class LayerSems:

    def __init__(self, sems, counts, layer):
        self.sems, self.counts, self.layer = sems, counts, layer

    def __getitem__(self, name):
        return self.sems[name]

    def value(self, name, n):
        return n + self.layer * self.counts[name]

    def wait(self, eng, name, n):
        gate(eng, self.sems[name], self.value(name, n))


def build(nc, io):
    with ExitStack() as ctx:
        def sb(name, shape, dt=F32):
            return ctx.enter_context(nc.sbuf_tensor(name, shape, dt))

        def sem(name):
            return ctx.enter_context(nc.semaphore(name))

        arena = sb("arena", [P, 51968])

        def area(start, *shape):
            n = 1
            for k in shape:
                n *= k
            flat = arena[:, start:start + n]
            if len(shape) == 1:
                return flat
            names = "abcd"[:len(shape)]
            return flat.rearrange(f"p ({' '.join(names)}) -> p {' '.join(names)}",
                                  **dict(zip(names[1:], shape[1:])))

        X = area(0, Q, D)
        M = area(0, G, Q * GS)
        Z = area(0, Q, D)
        U = area(8192, G, NC)
        ZT = area(8192, KT, TOK)
        XN = area(12800, G, Q, GS)
        E = area(12800, 2, PAIRS, BLK)
        K = area(12800, G, BLK)
        WIN = area(20992, PAIRS, 2, 2, SD)
        CA = area(29184, 2, PAIRS, Q + 1, GS)
        HP = area(38400, 2, PAIRS, NC)
        TMP = area(38400, PAIRS * BLK)
        TMPC = area(0, PAIRS * (Q + 1) * GS)
        TMPI = area(38400, PAIRS * (Q + 1) * GS)
        SKIP = area(12800, G, GS)[0:GS]
        CARRY = area(20992, 2, 2, PAIRS, CH // Q)
        ENDS = area(22016, 2, PAIRS, CH // Q)
        V = area(43008, 2, PAIRS, NC)
        BRAW = area(43008, 2, PAIRS, GS)
        CRAW = area(44032, 2, PAIRS, GS)
        GAIN0 = area(45056, D)
        SQ = area(46080, D)
        WGLU = area(12800, KT, 2 * D)
        H = area(38400, TILES, D)
        SG = area(43520, 2, D)

        WQ = [area(0, KT // 2, 2 * D), area(29184, KT // 2, 2 * D)]
        UROWS = area(8192, NU_RING, D)
        VROWS = [area(start, D) for start in (16384, 17408, 18432, 19456, 23552, 48640, 49664, 50688)]
        XCUR = area(20480, D)
        XNEXT = area(21504, D)
        XT = area(22528, KT, P)
        GAIN = area(47616, D)
        GAINF = area(0, D)
        YSQ = area(1024, D)
        SC = area(24576, 2, 2, NKEY)
        SC2 = area(25088, 2, NKEY)
        QN = area(25600, 2, 2 * P)
        QT = area(26112, 2, 2, P)
        CAND, CAND2 = area(26624, TOPK, TOPK), area(26880, TOPK, TOPK)
        EQ = area(27136, 2, TOPK, TOPK)
        FV = area(27648, HEADS, TOPK)
        EXPS = area(27776, HEADS, TOPK)
        GATE = area(28160, TILES * P)
        EID = area(37376, TILES * P).bitcast(U32)
        JUNK = area(43520, D).bitcast(BF16).rearrange("p (a b) -> p a b", a=2)
        DIAG = area(44544, 4, P)
        KEYS = area(45568, 2 * HEADS, NKEY)

        WQA = area(0, KT, D)
        WO = area(29184, KT, D)
        WKV = area(8192, KT, 2 * P)
        PB = area(10240, QPK, KVH, 2 * P)
        PT = area(16384, 2, QPK, KVH, P)
        SB = area(10240, NSEQ, WIDE)
        VBUF, KBUF = area(11776, NSEQ, P), area(12800, NSEQ, P)
        PTB, PTN = area(16384, NSEQ, P), area(17408, NSEQ, P)
        QBD, KBT = area(14336, NSEQ, P), area(19456, NSEQ, P)
        GKV, GMX = area(14336, D), area(15360, D)
        XK, XQ = area(20480, D), area(21504, D)
        XKT, XQT = area(22528, KT, P), area(23552, KT, P)
        QTA, QNA = area(24576, QPK, P), area(25600, D)
        OT = area(26624, QPK, P)
        KVN = area(27648, 2 * P)
        KZ = area(43520, KVH, P + TOK)
        V2 = area(44928, 2, P)
        KNT = area(45184, LAST)
        MASKS = area(45568, 2 * 2 * P)
        MASK1, MASKN = MASKS[:, 0:2 * P], MASKS[:, 2 * P:4 * P]
        SMASK = area(46080, NSEQ, WIDE)
        sinks = sb("sinks", [P, QPK * KVH + 1])
        mx = sb("mx", [P, 4, QH])

        top = sb("top", [P, 2, TOPK])
        topi = sb("topi", [P, 2, TOPK], U32)
        best_v = sb("best_v", [P, TOPK])
        best_i = sb("best_i", [P, TOPK], U32)
        ab = sb("ab", [P, 2, TOPK], U32)
        picked = sb("picked", [P, 2, TOPK])
        iota = sb("iota", [P, TOPK])
        idxu = sb("idxu", [P, 2, TOPK], U32)
        idxv = sb("idxv", [P, 2, TOPK], U32)
        hp = sb("hp", [P, 2, TOPK])
        ge = sb("ge", [P, 2, TOPK])
        av = sb("av", [P, 2, TOPK])
        sums = sb("sums", [P, 2, HEADS])
        rt = sb("rt", [P, 4])

        ident = sb("ident", [P, P])
        fold = sb("fold", [P, P])
        small = 47616

        def part(*shape):
            nonlocal small
            n = 1
            for k in shape:
                n *= k
            small += n
            return area(small - n, *shape)

        par = part(3, PAIRS)
        w = part(16, PAIRS)
        wi = part(PAIRS).bitcast(I32)
        pw = part(2, Q + 1, PAIRS)
        pwr = part(2, Q, PAIRS)
        Bb = part(2, PAIRS, GS)
        w8 = w.rearrange("p (r i) q -> p r i q", r=2)
        h0 = part(2, NSEQ, PAIRS)
        hs = part(2, NSEQ, PAIRS)
        hf = part(2, PAIRS)
        dsk = part(G)[0:GS]
        zero = part((Q - 1) * GS)[0:GS]
        st = part(4, Q)

        ps = ctx.enter_context(nc.psum_tensor("ps", [P, 8, 512], F32))

        x_in, gain_in, par_in = sem("x_in"), sem("gain_in"), sem("par_in")
        bc_in, ident_in, pad_out = sem("bc_in"), sem("ident_in"), sem("pad_out")
        fold_in, twice, router_gain_in = sem("fold_in"), sem("twice"), sem("router_gain_in")
        squares, roots_in, roots = sem("squares"), sem("roots_in"), sem("roots")
        normed, angles, sines = sem("normed"), sem("angles"), sem("sines")
        e_ready, ca_ready, zeroed = sem("e_ready"), sem("ca_ready"), sem("zeroed")
        powers_ready, s_pool = sem("powers_ready"), sem("s_pool")
        turned, turned_out = sem("turned"), sem("turned_out")
        skip_added, m_out, k_in = sem("skip_added"), sem("m_out"), sem("k_in")
        v_ready, v_act, v_dve = sem("v_ready"), sem("v_act"), sem("v_dve")
        scanned, y_ready, y_out = sem("scanned"), sem("y_ready"), sem("y_out")
        z_ready, z_act, z_dve = sem("z_ready"), sem("z_act"), sem("z_dve")
        glu_in, h_in, glu_ready = sem("glu_in"), sem("h_in"), sem("glu_ready")
        gate_ready, mixed = sem("gate_ready"), sem("mixed")
        states_out, state_ready = sem("states_out"), sem("state_ready")
        s_dve, s_act = sem("s_dve"), sem("s_act")
        wq_in, iota_in, sinks_in, gainf_in = sem("wq_in"), sem("iota_in"), sem("sinks_in"), sem("gainf_in")
        wa_in, wkv_in, buf_in, win_out = sem("wa_in"), sem("wkv_in"), sem("buf_in"), sem("win_out")
        y_ready2, y_stored = sem("y_ready2"), sem("y_stored")
        att_names = ("ms root x xt xt_copied kv kv_copied kt kt_copied q q_copied qt qt_copied s masked "
                     "max exps probs pt pt_act pt_dve o o_copied y added v_moved").split()
        att_sems = [{n: sem(f"{n}_{k}") for n in att_names} for k in ("prompt", "sample")]
        sample_q = sem("sample_q")
        last_ms, last_root = sem("last_ms"), sem("last_root")
        per_tile = "ms_ready root_ready x_ready x_cur xt_ready fv_ready exp_done gated h_done".split()
        per_head = "q_ready q_copied qt_ready qt_copied sc_ready sc_copied routed".split()
        per_slot = "idxu_ready idxv_ready gelus weights".split()
        counts = {"xt_copied": 2 * TILES, **dict.fromkeys(per_tile, TILES), **dict.fromkeys(per_head, HEADS * TILES),
                  **dict.fromkeys(per_slot, SLOTS), **dict.fromkeys(("diags", "products"), products_before(SLOTS)),
                  "dots": TOPK * SLOTS, "rows_added": len(DVE_ROWS) * PACKED}
        peer_sem = {n: sem(n) for n in counts}
        peer_sems = [LayerSems(peer_sem, counts, layer) for layer in range(2)]
        u_in = [sem(f"u_in{i}") for i in range(NU_RING)]
        v_in = [sem(f"v_in{i}") for i in range(NV_RING)]

        UR = [list(range(7 * r, min(7 * r + 7, G))) for r in range(-(-G // 7))]
        WR = [(ri, 4 * r) for ri in range(2) for r in range(PAIRS // 4)]
        NU, NW = len(UR), len(WR)
        PR = PAIRS // 4
        VR = [list(range(6 * r, min(6 * r + 6, PAIRS))) for r in range(-(-PAIRS // 6))]

        def v_copy(copy, r, pairs, ri, g2):
            n = len(pairs)
            b = 2 * (r % 4)
            half = n // 2
            src = ps[SD * ri:SD * ri + SD, b:b + 2, 0:half * 2 * NC].rearrange(
                "p a (q g n) -> p a q g n", g=2, n=NC)[:, :, :, g2, :]
            dst = V[SD * g2:SD * g2 + SD, ri, pairs[0]:pairs[0] + n, :].rearrange("p (a q) n -> p a q n", a=2)
            return copy(dst, src)

        def pt_copy(copy, r):
            return copy(PT[:, :, r, :, :], ps[:, r, :].rearrange("p (h k n) -> p h k n", h=2, k=2))

        def z_copy(copy, r):
            kt, half = r // 2, r % 2
            dst = ZT[:, kt, :].rearrange("p (c s) -> p s c", s=Q)[:, 4 * half:4 * half + 4, :]
            return copy(dst, ps[:, r % 4, 0:4 * NC].rearrange("p (s c) -> p s c", c=NC))

        def powers(t, ri, n):
            return t[:, ri].rearrange("p s q -> p q s").unsqueeze(3).to_broadcast([P, PAIRS, n, GS])

        def over(t, n):
            return t.unsqueeze(2).to_broadcast([P, PAIRS, n, GS])

        block = ctx.enter_context(nc.Block())

        @block.sync
        def _(sp):
            sp.dma_start(par[:, :, :], io["s5par"]).then_inc(par_in, 16)
            sp.dma_start(ident[:, :], io["ident"]).then_inc(ident_in, 16)
            sp.dma_start(arena[0:NC, 0:Q * D], io["x"].rearrange("(c s) d -> c (s d)", s=Q)).then_inc(x_in, 16)
            sp.dma_start(GAIN0, io["gains"][0:1, :].partition_broadcast(P)).then_inc(gain_in, 16)
            sp.dma_start(BRAW, io["s5b"]).then_inc(bc_in, 16)
            sp.dma_start(CRAW, io["s5c"]).then_inc(bc_in, 16)
            sp.dma_start(h0[:, :, :, :], io["h0"]).then_inc(bc_in, 16)
            sp.dma_start(dsk[:, :], io["dskip"]).then_inc(bc_in, 16)
            sp.dma_start(fold[:, :], io["fold"]).then_inc(fold_in, 16)
            sp.wait_ge(zeroed, 1)
            mp = io["kern"].rearrange("g j n -> j g n")
            sp.dma_start(mp[:, :, 0:(Q - 1) * GS],
                         zero[:, :].unsqueeze(1).to_broadcast([GS, G, (Q - 1) * GS])).then_inc(pad_out, 16)
            sp.wait_ge(skip_added, 1)
            sp.dma_start(mp[:, :, (Q - 1) * GS:], M[0:GS, :, :]).then_inc(m_out, 16)
            sp.wait_ge(pad_out, 16)
            sp.wait_ge(m_out, 16)
            sp.wait_ge(turned, NU + NW)
            for s in range(Q):
                a = (Q - 1 - s) * GS
                sp.dma_start(K[GS * s:GS * s + GS, :, :], mp[:, :, a:a + BLK]).then_inc(k_in, 16)
            glu = io["w_glu"].rearrange("(k p) n -> p k n", p=P)
            sp.wait_ge(state_ready, 2)
            sp.dma_start(WGLU[:, 4:8, :], glu[:, 4:8, :]).then_inc(glu_in, 16)
            sp.dma_start(io["hs"], hs[:, :, :, :]).then_inc(states_out, 16)
            sp.dma_start(io["hf"], hf[:, :, :]).then_inc(states_out, 16)
            sp.wait_ge(y_ready, PR)
            sp.dma_start(WGLU[:, 0:4, :], glu[:, 0:4, :]).then_inc(glu_in, 16)
            sp.dma_start(H[:, 0:FULL, :], io["x"][0:SEQ, :].rearrange("(t p) d -> p t d", p=P)).then_inc(h_in, 16)
            sp.dma_start(H[0:LAST, FULL, :], io["x"][SEQ:TOK, :]).then_inc(h_in, 16)
            sp.dma_start(iota[:, :], io["iota"]).then_inc(iota_in, 16)
            sp.dma_start(GAIN, io["gains"][2:3, :].partition_broadcast(P)).then_inc(router_gain_in, 16)
            sp.dma_start(KEYS, io["keys"][0]).then_inc(wq_in, 16)
            wq = io["peer_wq"]
            sp.wait_ge(z_ready, 2 * KT)
            for i in range(2):
                sp.dma_start(WQ[i], wq[0].rearrange("(k p) n -> p k n", p=P)[:, 4 * i:4 * i + 4, :]).then_inc(wq_in, 16)
            sp.wait_ge(mixed, TILES)
            sp.dma_start(H[LAST:P, FULL, :], H[0:LAST, FULL, :]).then_inc(twice, 16)
            sp.dma_start(sinks[:, :], io["sinks"]).then_inc(sinks_in, 16)
            S = peer_sems[0]
            S.wait(sp, "q_ready", HEADS * TILES)
            sp.dma_start(WQA, io["w_q"].rearrange("(k p) n -> p k n", p=P)).then_inc(wa_in, 16)
            sp.dma_start(WO, io["w_o"].rearrange("(k p) n -> p k n", p=P)).then_inc(wa_in, 16)
            S.wait(sp, "sc_ready", HEADS * TILES)
            sp.dma_start(MASKS, io["masks"]).then_inc(wa_in, 16)
            sp.dma_start(SMASK, io["smask"]).then_inc(wa_in, 16)
            S.wait(sp, "x_ready", TILES)
            sp.dma_start(GAIN, io["gains"][3:4, :].partition_broadcast(P)).then_inc(router_gain_in, 16)
            S.wait(sp, "dots", TOPK * SLOTS)
            sp.dma_start(WKV, io["w_kv"].rearrange("(k p) n -> p k n", p=P)).then_inc(wkv_in, 16)
            sp.dma_start(GKV, io["gains"][4:5, :].partition_broadcast(P)).then_inc(wkv_in, 16)
            sp.dma_start(GMX, io["gains"][1:2, :].partition_broadcast(P)).then_inc(wkv_in, 16)
            sp.dma_start(io["kv_s"][0, :, 0:P - STEPS, :], io["k_buf"][:, STEPS:P, :]).then_inc(win_out, 16)
            sp.dma_start(io["kv_s"][1, :, 0:P - STEPS, :], io["v_buf"][:, STEPS:P, :]).then_inc(win_out, 16)
            A, B = att_sems
            sp.wait_ge(A["kv_copied"], 2 * FULL)
            sp.dma_start(io["kv_p"], KVN).then_inc(win_out, 16)
            sp.wait_ge(A["pt"], QPK * FULL)
            sp.dma_start(KBUF, io["k_buf"].rearrange("b j n -> j b n")).then_inc(buf_in, 16)
            sp.dma_start(VBUF, io["v_buf"].rearrange("b j n -> j b n")).then_inc(buf_in, 16)
            sp.wait_ge(A["kv_copied"], 2 * FULL + 1)
            for i in range(2):
                sp.dma_start(io["kv_s"][i, :, P - STEPS:P, :], KVN[0:LAST, i * P:(i + 1) * P]).then_inc(win_out, 16)
            sp.wait_ge(A["q"], TILES)
            sp.dma_start(WQ[0], wq[1].rearrange("(k p) n -> p k n", p=P)[:, 0:4, :]).then_inc(wq_in, 16)
            sp.wait_ge(B["masked"], NSEQ // 2)
            sp.dma_start(KEYS, io["keys"][1]).then_inc(wq_in, 16)
            sp.wait_ge(B["y"], 1)
            sp.wait_ge(win_out, 16 * 5)
            sp.dma_start(WQ[1], wq[1].rearrange("(k p) n -> p k n", p=P)[:, 4:8, :]).then_inc(wq_in, 16)
            sp.wait_ge(B["added"], 1)
            sp.dma_start(H[LAST:P, FULL, :], H[0:LAST, FULL, :]).then_inc(twice, 16)
            peer_sems[1].wait(sp, "routed", HEADS * TILES)
            sp.dma_start(GAINF, io["gains"][5:6, :].partition_broadcast(P)).then_inc(gainf_in, 16)
            for t in range(TILES):
                n = P if t < FULL else LAST
                sp.wait_ge(y_ready2, t + 1)
                sp.dma_start(io["y"][t * P:t * P + n, :], H[0:n, t, :]).then_inc(y_stored, 16)
            sp.wait_ge(y_stored, 16 * TILES)
            sp.wait_ge(states_out, 32)

        @block.vector
        def _(dve):
            c = Chain(dve, s_dve)

            def mul(out, a, b):
                return dve.tensor_tensor(out, a, b, ALU.mult)

            def times(out_re, out_im, x_re, x_im, y_re, y_im, t1, t2):
                c(mul(t1, x_re, y_re))
                c(mul(t2, x_im, y_im))
                c(dve.tensor_tensor(out_re, t1, t2, ALU.subtract))
                c(mul(t1, x_re, y_im))
                c(mul(t2, x_im, y_re))
                c(dve.tensor_tensor(out_im, t1, t2, ALU.add))

            def exact_exp(out, x):
                k, r, q = w[:, 13, :], w[:, 14, :], w[:, 15, :]
                c(dve.tensor_scalar(x, x, -87.0, 88.0, ALU.max, ALU.min))
                c(dve.tensor_scalar(k, x, 1.4426950408889634, 12582912.0, ALU.mult, ALU.add))
                c(dve.tensor_scalar(k, k, -12582912.0, None, ALU.add))
                c(dve.scalar_tensor_tensor(r, k, -0.693359375, x, ALU.mult, ALU.add))
                c(dve.scalar_tensor_tensor(r, k, 2.12194440e-4, r, ALU.mult, ALU.add))
                c(dve.tensor_scalar(q, r, 1 / 5040, None, ALU.mult))
                for coef in (1 / 720, 1 / 120, 1 / 24, 1 / 6, 1 / 2, 1.0):
                    c(dve.scalar_tensor_tensor(q, q, coef, r, ALU.add, ALU.mult))
                c(dve.tensor_scalar(q, q, 1.0, None, ALU.add))
                c(dve.tensor_scalar(wi[:, :], k, 127.0, 8388608.0, ALU.add, ALU.mult))
                c(mul(out, q, wi.bitcast(F32)))

            def rsqrt_refined(r, root, v, t):
                c(dve.reciprocal(r, root))
                c(mul(t, r, r))
                c(mul(t, t, v))
                c(dve.tensor_scalar(t, t, -0.5, 1.5, ALU.mult, ALU.add))
                c(mul(r, r, t))

            dve.memset(zero[:, :], 0.0).then_inc(zeroed, 1)
            dve.wait_ge(par_in, 16)
            lr, li = par[:, 0, :], par[:, 1, :]
            dt, mag = w[:, 0, :], w[:, 1, :]
            exact_exp(dt, par[:, 2, :])
            c(mul(w[:, 2, :], li, dt))
            c(dve.tensor_scalar(w[:, 3, :], w[:, 2, :], 1 / (2 * PI), 12582912.0, ALU.mult, ALU.add))
            c(dve.tensor_scalar(w[:, 3, :], w[:, 3, :], -12582912.0, None, ALU.add))
            c1 = 6.28125
            c2 = int((2 * PI - c1) * 2 ** 20) / 2 ** 20
            for part in (c1, c2, 2 * PI - c1 - c2):
                c(dve.scalar_tensor_tensor(w[:, 2, :], w[:, 3, :], -part, w[:, 2, :], ALU.mult, ALU.add))
            c(dve.tensor_scalar(w[:, 5, :], w[:, 2, :], 3.1415925, -3.1415925, ALU.min, ALU.max))
            c(dve.scalar_tensor_tensor(w[:, 4, :], w[:, 5, :], -1.0, w[:, 5, :], ALU.mult, ALU.max))
            dve.tensor_scalar(w[:, 4, :], w[:, 4, :], -1.0, PI / 2, ALU.mult, ALU.add).then_inc(angles, 1)
            c(mul(w[:, 8, :], lr, dt))
            exact_exp(mag, w[:, 8, :])
            dve.wait_ge(squares, 1)
            dve.tensor_scalar(st[0:NC, 1, :], st[0:NC, 0, :], 1.0 / D, EPS, ALU.mult, ALU.add).then_inc(roots_in, 1)
            dve.wait_ge(roots, 1)
            rsqrt_refined(st[0:NC, 3, :], st[0:NC, 2, :], st[0:NC, 1, :], st[0:NC, 0, :])
            dve.wait_ge(gain_in, 16)
            for s in range(Q):
                rows = X[0:NC, s, :].rearrange("p (g j) -> p g j", j=GS)
                gain = GAIN0[0:NC, :].rearrange("p (g j) -> p g j", j=GS)
                dve.scalar_tensor_tensor(XN[0:NC, :, s, :], rows, st[0:NC, 3, s:s + 1], gain,
                                         ALU.mult, ALU.mult).then_inc(normed, 1)

            dve.wait_ge(sines, 1)
            c(mul(pw[:, 0, 1, :], w[:, 6, :], mag))
            c(mul(pw[:, 1, 1, :], w[:, 7, :], mag))
            c(dve.memset(pw[:, 0, 0, :], 1.0))
            c(dve.memset(pw[:, 1, 0, :], 0.0))
            for have in (1, 2, 4):
                x, y = pw[:, :, 1:have + 1, :], pw[:, :, have, :].unsqueeze(2).to_broadcast([P, 2, have, PAIRS])
                t1, t2 = w[:, 8:8 + have, :], w[:, 12:12 + have, :]
                times(pw[:, 0, have + 1:2 * have + 1, :], pw[:, 1, have + 1:2 * have + 1, :],
                      x[:, 0], x[:, 1], y[:, 0], y[:, 1], t1, t2)
            dve.engine_nop().then_inc(powers_ready, 1)
            for s in range(Q):
                c(dve.tensor_copy(pwr[:, :, s, :], pw[:, :, Q - 1 - s, :]))
            ar1, t1, t2, fr, fi, rden = (w[:, i, :] for i in range(2, 8))
            c(dve.tensor_scalar(ar1, pw[:, 0, 1, :], -1.0, None, ALU.add))
            c(mul(t1, lr, lr))
            c(mul(t2, li, li))
            c(dve.tensor_tensor(rden, t1, t2, ALU.add))
            c(dve.reciprocal(rden, rden))
            c(mul(t1, ar1, lr))
            c(mul(t2, pw[:, 1, 1, :], li))
            c(dve.tensor_tensor(fr, t1, t2, ALU.add))
            c(mul(fr, fr, rden))
            c(mul(t1, pw[:, 1, 1, :], lr))
            c(mul(t2, ar1, li))
            c(dve.tensor_tensor(fi, t1, t2, ALU.subtract))
            c(mul(fi, fi, rden))
            dve.wait_ge(bc_in, 64)
            bc = [P, PAIRS, GS]
            u1, u2 = (TMP[:, i * 512:(i + 1) * 512].rearrange("p (a b) -> p a b", b=GS) for i in range(2))
            times(Bb[:, 0], Bb[:, 1], BRAW[:, 0], BRAW[:, 1],
                  fr.unsqueeze(2).to_broadcast(bc), fi.unsqueeze(2).to_broadcast(bc), u1, u2)
            dve.wait_ge(turned, NU)
            tE = TMP[:, 0:PAIRS * BLK].rearrange("p (q s j) -> p q s j", s=Q, j=GS)
            for ri in range(2):
                out = E[:, ri].rearrange("p q (s j) -> p q s j", j=GS)
                c(mul(out, powers(pwr, 0, Q), over(Bb[:, ri], Q)))
                c(mul(tE, powers(pwr, 1, Q), over(Bb[:, 1 - ri], Q)))
                dve.tensor_tensor(E[:, ri].rearrange("p q n -> p (q n)"), E[:, ri].rearrange("p q n -> p (q n)"),
                                  TMP[:, 0:PAIRS * BLK], ALU.add if ri else ALU.subtract).then_inc(e_ready, 1)
                dve.wait_ge(e_ready, ri + 1)
            c(mul(CA[:, 1], powers(pw, 0, Q + 1), over(CRAW[:, 1], Q + 1)))
            c(mul(TMPI.rearrange("p (q s j) -> p q s j", s=Q + 1, j=GS), powers(pw, 1, Q + 1),
                  over(CRAW[:, 0], Q + 1)))
            flat = CA[:, 1].rearrange("p q s j -> p (q s j)")
            c(dve.scalar_tensor_tensor(flat, flat, -1.0, TMPI, ALU.mult, ALU.subtract))
            dve.engine_nop().then_inc(ca_ready, 1)
            c(dve.tensor_copy(w8[:, :, 0, :], pw[:, :, Q, :]))
            for have in (1, 2, 4):
                x, y = w8[:, :, 0:have, :], w8[:, :, have - 1, :].unsqueeze(2).to_broadcast([P, 2, have, PAIRS])
                times(w8[:, 0, have:2 * have, :], w8[:, 1, have:2 * have, :], x[:, 0], x[:, 1], y[:, 0], y[:, 1],
                      pwr[:, 0, 0:have, :], pwr[:, 1, 0:have, :])
            c(dve.memset(HP[:, :, :, 0], 0.0))
            c(dve.tensor_copy(HP[:, :, :, CH:NC], h0.rearrange("p r b q -> p r q b")))
            dve.wait_ge(ca_ready, 2)
            for r, pairs in enumerate(VR):
                dve.wait_ge(v_ready, r + 1)
                for g2 in range(2):
                    v_copy(dve.tensor_copy, r, pairs, 1, g2).then_inc(v_dve, 1)

            dve.wait_ge(v_dve, 2 * len(VR))
            dve.wait_ge(v_act, 2 * len(VR))

            def carry(out, now, v_in, power):
                n = out.shape[3]
                full = [P, 2, 2, PAIRS, n]
                factor = w8[:, :, power - 1, :].unsqueeze(2).unsqueeze(4).to_broadcast(full)
                products = CARRY[:, :, :, :, 0:n]
                for i in range(2):
                    ins = mul(products[:, i], factor[:, i], now)
                c(ins)
                c(dve.tensor_tensor(out, v_in, products[:, 0], ALU.add))
                dve.tensor_tensor(out[:, 0], out[:, 0], products[:, 1, 1], ALU.subtract)
                c(dve.tensor_tensor(out[:, 1], out[:, 1], products[:, 1, 0], ALU.add))

            runs = CH // Q
            HR = HP[:, :, :, 0:CH].rearrange("p r q (a i) -> p r q a i", i=Q)
            VC = V[:, :, :, 0:CH].rearrange("p r q (a i) -> p r q a i", i=Q)
            c(dve.tensor_copy(HR[:, :, :, :, 1], VC[:, :, :, :, 0]))
            for i in range(1, Q):
                carry(HR[:, :, :, :, i + 1] if i < Q - 1 else ENDS, HR[:, :, :, :, i], VC[:, :, :, :, i], 1)
            c(dve.memset(HR[:, :, :, 0, 0], 0.0))
            for a in range(runs):
                out = HR[:, :, :, a + 1:a + 2, 0] if a < runs - 1 else hf.unsqueeze(3)
                carry(out, HR[:, :, :, a:a + 1, 0], ENDS[:, :, :, a:a + 1], Q)
            for i in range(1, Q):
                carry(HR[:, :, :, :, i], HR[:, :, :, :, 0], HR[:, :, :, :, i], i)
            dve.engine_nop().then_inc(scanned, 1)
            carry(hs.rearrange("p r b q -> p r q b"), h0.rearrange("p r b q -> p r q b"), V[:, :, :, CH:NC], 1)
            dve.engine_nop().then_inc(state_ready, 2)

            for r in range(1, 2 * KT, 2):
                dve.wait_ge(z_ready, r + 1)
                z_copy(dve.tensor_copy, r).then_inc(z_dve, 1)
            dve.wait_ge(y_ready, PR)
            dve.wait_ge(h_in, 32)
            for t in range(TILES):
                n = P if t < FULL else LAST
                dve.wait_ge(gate_ready, t + 1)
                gl = ps[0:n, 4 * (t % 2):4 * (t % 2) + 2, :].rearrange("p a b -> p (a b)")
                c(mul(SG[0:n, t % 2, :], SG[0:n, t % 2, :], gl))
                dve.tensor_tensor(H[0:n, t, :], H[0:n, t, :], SG[0:n, t % 2, :], ALU.add).then_inc(mixed, 1)

            def peer(L):
                S = peer_sems[L]

                def mean_square(t):
                    c(dve.scalar_tensor_tensor(XNEXT, H[:, t, :], 1.0, H[:, t, :], ALU.mult, ALU.mult,
                                               accum_out=rt[:, 0:1]))
                    dve.tensor_scalar(rt[:, 0:1], rt[:, 0:1], 1.0 / D, EPS, ALU.mult, ALU.add).then_inc(S["ms_ready"], 1)

                def normalise(t):
                    S.wait(dve, "root_ready", t + 1)
                    rsqrt_refined(rt[:, 2:3], rt[:, 1:2], rt[:, 0:1], rt[:, 3:4])
                    S.wait(dve, "xt_ready", t)
                    dve.scalar_tensor_tensor(XNEXT, H[:, t, :], rt[:, 2:3], GAIN, ALU.mult, ALU.mult)\
                       .then_inc(S["x_ready"], 1)

                def best(par, r, half):
                    if half == 0:
                        S.wait(dve, "sc_copied", r + 1)
                    sc, sc2, v, i = SC[:, par, half, :], SC2[:, half, :], top[:, half, :], topi[:, half, :]
                    c(dve.max(v[:, 0:8], sc))
                    c(dve.max_index(i[:, 0:8], v[:, 0:8], sc))
                    c(dve.match_replace(sc2, v[:, 0:8], sc, LOWEST))
                    c(dve.max(v[:, 8:16], sc2))
                    c(dve.max_index(i[:, 8:16], v[:, 8:16], sc2))

                def best_of_both(par, r):
                    S.wait(dve, "sc_copied", r + 1)
                    both = [(SC[:, par, i, :], SC2[:, i, :], top[:, i, :], topi[:, i, :]) for i in range(2)]
                    for step in (lambda sc, sc2, v, i: dve.max(v[:, 0:8], sc),
                                 lambda sc, sc2, v, i: dve.max_index(i[:, 0:8], v[:, 0:8], sc),
                                 lambda sc, sc2, v, i: dve.match_replace(sc2, v[:, 0:8], sc, LOWEST),
                                 lambda sc, sc2, v, i: dve.max(v[:, 8:16], sc2),
                                 lambda sc, sc2, v, i: dve.max_index(i[:, 8:16], v[:, 8:16], sc2)):
                        for half in both:
                            ins = step(*half)
                        c(ins)

                def merge():
                    c(dve.tensor_tensor(CAND, top[:, 0, :].unsqueeze(2).to_broadcast([P, TOPK, TOPK]),
                                        top[:, 1, :].unsqueeze(1).to_broadcast([P, TOPK, TOPK]), ALU.add))
                    cand, cand2 = (x.rearrange("p a b -> p (a b)") for x in (CAND, CAND2))
                    c(dve.max(best_v[:, 0:8], cand))
                    c(dve.max_index(best_i[:, 0:8], best_v[:, 0:8], cand))
                    c(dve.match_replace(cand2, best_v[:, 0:8], cand, LOWEST))
                    c(dve.max(best_v[:, 8:16], cand2))
                    c(dve.max_index(best_i[:, 8:16], best_v[:, 8:16], cand2))

                def name_experts(r, h):
                    c(dve.tensor_scalar(ab[:, 0, :], best_i[:, :], 4, None, ALU.logical_shift_right))
                    c(dve.tensor_scalar(ab[:, 1, :], best_i[:, :], 15, None, ALU.bitwise_and))
                    full = [P, 2, TOPK, TOPK]
                    c(dve.tensor_tensor(EQ, ab[:, :, :].unsqueeze(3).to_broadcast(full),
                                        iota[:, :].unsqueeze(1).unsqueeze(1).to_broadcast(full), ALU.is_equal))
                    c(mul(EQ, EQ, topi[:, :, :].unsqueeze(2).to_broadcast(full)))
                    c(dve.tensor_reduce(picked[:, :, :], EQ, AX.X, ALU.add))
                    c(dve.scalar_tensor_tensor(EID[:, bass.ds(r * TOPK, TOPK)], picked[:, 0, :], float(NKEY),
                                               picked[:, 1, :], ALU.mult, ALU.add))
                    dve.tensor_copy(FV[:, bass.ds(h, 1), :], best_v[:, :].unsqueeze(1)).then_inc(S["routed"], 1)

                def softmax(t):
                    S.wait(dve, "routed", 8 * t + 8)
                    dve.tensor_tensor(EXPS, FV, FV[:, :, 0:1].to_broadcast([P, HEADS, TOPK]), ALU.subtract)\
                       .then_inc(S["fv_ready"], 1)
                    S.wait(dve, "exp_done", t + 1)
                    c(dve.tensor_reduce(sums[:, 0, :], EXPS, AX.X, ALU.add))
                    c(dve.reciprocal(sums[:, 1, :], sums[:, 0, :]))
                    dve.tensor_tensor(GATE[:, bass.ds(t * P, P)].rearrange("p (h k) -> p h k", k=TOPK), EXPS,
                                      sums[:, 1, :].unsqueeze(2).to_broadcast([P, HEADS, TOPK]), ALU.mult)\
                       .then_inc(S["gated"], 1)
                    S.wait(dve, "gated", t + 1)

                def each_half(j):
                    if isinstance(j, int) and j >= PACKED:
                        return [(slice(0, LAST), j * TOPK), (slice(LAST, P), (j + HEADS // 2) * TOPK)]
                    return [(slice(0, P), j * TOPK)]

                def stage_u(j, par):
                    halves = each_half(j)
                    if not isinstance(j, int):
                        halves = [(slice(0, LAST), j * TOPK),
                                  (slice(LAST, P), (j + (j // PACKED) * (HEADS // 2)) * TOPK)]
                    for rows, at in halves:
                        ins = dve.tensor_copy(idxu[rows, par, :], EID[rows, bass.ds(at, TOPK)])
                    ins.then_inc(S["idxu_ready"], 1)

                def stage_v(j, par):
                    S.wait(dve, "products", products_before(j - 1))
                    for rows, at in each_half(j):
                        ins = dve.tensor_copy(idxv[rows, par, :], EID[rows, bass.ds(at, TOPK)])
                    ins.then_inc(S["idxv_ready"], 1)

                def weigh(j, par):
                    S.wait(dve, "diags", products_before(j - 1))
                    S.wait(dve, "gelus", j + 1)
                    for rows, at in each_half(j):
                        ins = dve.tensor_tensor(av[rows, par, :], ge[rows, par, :], GATE[rows, bass.ds(at, TOPK)], ALU.mult)
                    ins.then_inc(S["weights"], 1)

                def dot(j, par, k):
                    gate(dve, u_in[k % NU_RING], 16 * (2 * j + k // NU_RING + 1) + L * 16 * 2 * SLOTS)
                    S.wait(dve, "dots", 16 * j + k - 1)
                    dve.tensor_tensor_reduce(JUNK[:, k % 2, :], UROWS[:, k % NU_RING, :], XCUR, 1.0, 0.0,
                                             ALU.mult, ALU.add, hp[:, par, k:k + 1]).then_inc(S["dots"], 1)

                def add_row(t, j, par, k):
                    i = DVE_ROWS.index(k)
                    if i == 0:
                        S.wait(dve, "weights", j + 1)
                    S.wait(dve, "rows_added", len(DVE_ROWS) * j + i)
                    gate(dve, v_in[k % NV_RING], 16 * (2 * j + k // NV_RING + 1) + L * 16 * 2 * SLOTS)
                    row = H[:, bass.ds(t, 1), :].rearrange("p a d -> p (a d)")
                    dve.scalar_tensor_tensor(row, VROWS[k % NV_RING], av[:, par, k:k + 1], row,
                                             ALU.mult, ALU.add).then_inc(S["rows_added"], 1)

                def finish(t, j):
                    S.wait(dve, "products", products_before(j))
                    S.wait(dve, "rows_added", len(DVE_ROWS) * min(j, PACKED) if isinstance(j, int) else len(DVE_ROWS) * j)
                    row = H[:, bass.ds(t, 1), :].rearrange("p a d -> p (a d)")
                    dve.tensor_tensor(row, row, ps[:, 0:2, :].rearrange("p a b -> p (a b)"), ALU.add)\
                       .then_inc(S["h_done"], 1)

                def slot(t, h, par, route, first_head, first, last):
                    j = t * 8 + h
                    r = j + 8
                    adds = not first and len(pe_rows(j - 1)) < TOPK
                    before = t - 1 if first_head else t

                    def dots(a, b):
                        for k in range(a, b):
                            dot(j, par, k)
                            for kv in DVE_ROWS:
                                if adds and k == min(kv + 1, TOPK - 1):
                                    add_row(before, j - 1, 1 - par, kv)

                    c.reset()
                    if first_head:
                        S.wait(dve, "x_ready", t + 1)
                        dve.tensor_copy(XCUR, XNEXT).then_inc(S["x_cur"], 1)
                        S.wait(dve, "x_cur", t + 1)
                        if route:
                            mean_square(t + 1)
                    if not last:
                        stage_u(j + 1, 1 - par)
                    dots(0, 2)
                    if not first:
                        weigh(j - 1, 1 - par)
                    dots(2, 6)
                    if route and first_head:
                        normalise(t + 1)
                    if not (first and first_head):
                        stage_v(j, par)
                    dots(6, 8)
                    if route and not first_head:
                        best(par, r, 0)
                    dots(8, 10)
                    if route and not first_head:
                        best(par, r, 1)
                    dots(10, 13)
                    if route and not first_head:
                        merge()
                    dots(13, 16)
                    if first_head and not first:
                        finish(t - 1, j)
                    if route and first_head:
                        best(par, r, 0)
                        best(par, r, 1)
                        merge()
                    if route:
                        name_experts(r, h)

                def tile(t, route, first):
                    for par in range(2):
                        slot(t, par, par, route, par == 0, first and par == 0, False)
                    if route:
                        with dve.Fori(1, HEADS // 2) as m:
                            for par in range(2):
                                slot(t, 2 * m + par, par, route, False, False, False)
                        softmax(t + 1)
                    else:
                        for h in range(2, HEADS // 2):
                            slot(t, h, h % 2, route, False, False, h == HEADS // 2 - 1)

                mean_square(0)
                dve.wait_ge(router_gain_in, 16 * (L + 1))
                dve.wait_ge(iota_in, 16)
                normalise(0)

                def route_first(h, par):
                    best_of_both(par, h)
                    merge()
                    name_experts(h, h)

                c.reset()
                route_first(0, 0)
                stage_u(0, 0)
                stage_v(0, 0)
                route_first(1, 1)
                c.reset()
                with dve.Fori(1, HEADS // 2) as m:
                    for par in range(2):
                        route_first(2 * m + par, par)
                    c.reset()
                softmax(0)
                tile(0, True, True)
                dve.wait_ge(twice, 16 * (L + 1))
                with dve.Fori(1, FULL) as t:
                    tile(t, True, False)
                tile(FULL, False, False)
                weigh(SLOTS - 1, 1)
                finish(FULL, SLOTS)

            def probabilities(S, t, rows, n):
                gate(dve, S["exps"], t + 1)
                c(dve.tensor_tensor(mx[:, 2, 0:n], mx[:, 2, 0:n], mx[:, 3, 0:n], ALU.add))
                c(dve.reciprocal(mx[:, 2, 0:n], mx[:, 2, 0:n]))
                dve.tensor_tensor(rows, rows, mx[:, 2, 0:n].unsqueeze(2).to_broadcast(rows.shape), ALU.mult)\
                   .then_inc(S["probs"], 1)

            def row_max(S, t, rows, n, sink):
                gate(dve, S["masked"], (t + 1) * (QPK if n == QH else NSEQ // 2))
                c(dve.tensor_reduce(mx[:, 0, 0:n], rows, AX.X, ALU.max))
                c(dve.tensor_tensor(mx[:, 0, 0:n], mx[:, 0, 0:n], sink, ALU.max))
                c(dve.tensor_tensor(mx[:, 1, 0:n], sink, mx[:, 0, 0:n], ALU.subtract))
                dve.tensor_scalar(mx[:, 0, 0:n], mx[:, 0, 0:n], -1.0, None, ALU.mult).then_inc(S["max"], 1)

            def att_norm(S, t, tile):
                gate(dve, S["xt"], 2 * t)
                c(dve.scalar_tensor_tensor(XK, H[:, tile, :], 1.0, H[:, tile, :], ALU.mult, ALU.mult,
                                           accum_out=rt[:, 0:1]))
                dve.tensor_scalar(rt[:, 0:1], rt[:, 0:1], 1.0 / D, EPS, ALU.mult, ALU.add).then_inc(S["ms"], 1)
                gate(dve, S["root"], t + 1)
                rsqrt_refined(rt[:, 2:3], rt[:, 1:2], rt[:, 0:1], rt[:, 3:4])
                for out, gain in ((XK, GKV), (XQ, GMX)):
                    dve.scalar_tensor_tensor(out, H[:, tile, :], rt[:, 2:3], gain, ALU.mult, ALU.mult)\
                       .then_inc(S["x"], 1)

            def add_output(S, t, tile, n):
                gate(dve, S["y"], t + 1)
                flat = H[0:n, bass.ds(tile, 1), :].rearrange("p a d -> p (a d)")
                dve.tensor_tensor(flat, flat, ps[0:n, 4:6, :].rearrange("p a b -> p (a b)"), ALU.add)\
                   .then_inc(S["added"], 1)

            def att_keys(S, t):
                gate(dve, S["kt"], t + 1)
                for kvh in range(KVH):
                    rows = slice(kvh * HD, kvh * HD + HD)
                    dve.tensor_copy(KZ[rows, kvh, bass.ds(P + t * P, P)], ps[rows, 3, 0:P]).then_inc(S["kt_copied"], 1)

            def sample_queries():
                dve.wait_ge(att_sems[0]["qt"], TILES)
                for kvh in range(KVH):
                    rows = slice(kvh * HD, kvh * HD + HD)
                    for half in range(2):
                        out = QBD[rows, :, kvh * HD:kvh * HD + HD].rearrange("p b (i s) -> p i b s", s=STEPS)
                        dve.tensor_copy(out[:, 4 * half:4 * half + 4],
                                        ps[rows, 6 + half, :].rearrange("p (i n) -> p i n", i=4)[:, :, 0:LAST]
                                        .rearrange("p i (b s) -> p i b s", s=STEPS)).then_inc(sample_q, 1)

            def att_tile(t, mask, more):
                S = att_sems[0]
                c.reset()
                for i in range(QPK):
                    gate(dve, S["s"], QPK * t + i + 1)
                    dve.scalar_tensor_tensor(PB[:, i], ps[:, i % 4, :].rearrange("p (a b) -> p a b", a=2), SCALE,
                                             mask.unsqueeze(1).to_broadcast([P, 2, 2 * P]), ALU.mult, ALU.add)\
                       .then_inc(S["masked"], 1)
                rows = PB.rearrange("p a b n -> p (a b) n")
                row_max(S, t, rows, QH, sinks[:, 0:QH])
                if more:
                    att_keys(S, t + 1)
                else:
                    dve.wait_ge(S["kt"], TILES)
                    dve.tensor_copy(KNT, ps[:, 3, 0:LAST]).then_inc(att_sems[1]["kt_copied"], 1)
                    c(dve.memset(QBD, 0.0))
                probabilities(S, t, rows, QH)
                if more:
                    att_norm(S, t + 2, t + 2)
                else:
                    sample_queries()
                for r in range(1, QPK, 2):
                    gate(dve, S["pt"], QPK * t + r + 1)
                    pt_copy(dve.tensor_copy, r).then_inc(S["pt_dve"], 1)
                gate(dve, S["o"], t + 1)
                for kvh in range(KVH):
                    rows = slice(kvh * HD, kvh * HD + HD)
                    dve.tensor_copy(OT[rows, :, :].rearrange("p (a i) n -> p a i n", a=4),
                                    ps[rows, 0:4, :].rearrange("p a (i k n) -> p a i k n", i=2, k=2)[:, :, :, kvh, :])\
                       .then_inc(S["o_copied"], 1)
                add_output(S, t, t, P)
                gate(dve, S["added"], t + 1)

            def attention():
                peer_sems[0].wait(dve, "h_done", TILES)
                c(dve.memset(KZ, 0.0))
                c(dve.memset(V2[:, 0, :], 0.0))
                dve.wait_ge(wkv_in, 48)
                dve.wait_ge(wa_in, 64)
                dve.wait_ge(sinks_in, 16)
                att_norm(att_sems[0], 0, 0)
                att_keys(att_sems[0], 0)
                att_norm(att_sems[0], 1, 1)
                att_tile(0, MASK1, True)
                with dve.Fori(1, FULL - 1) as t:
                    att_tile(t, MASKN, True)
                att_tile(FULL - 1, MASKN, False)
                S = att_sems[1]
                c.reset()
                for r in range(NSEQ // 2):
                    dve.wait_ge(S["s"], r + 1)
                    dve.scalar_tensor_tensor(SB[:, 2 * r:2 * r + 2, :],
                                             ps[:, r, 0:2 * WIDE].rearrange("p (a b) -> p a b", a=2), SCALE,
                                             SMASK[:, 2 * r:2 * r + 2, :], ALU.mult, ALU.add).then_inc(S["masked"], 1)
                row_max(S, 0, SB, NSEQ, sinks[:, QH:QH + 1].to_broadcast([P, NSEQ]))
                probabilities(S, 0, SB, NSEQ)
                dve.wait_ge(S["o"], 1)
                for kvh in range(KVH):
                    rows = slice(kvh * HD, kvh * HD + HD)
                    for half in range(2):
                        src = ps[rows, 4 + half, :].rearrange("p (b k i s) -> p k i b s", b=4, k=2, s=STEPS)[:, kvh]
                        dst = OT[rows, :, 0:LAST].rearrange("p i (b s) -> p i b s", s=STEPS)
                        dve.tensor_copy(dst[:, :, 4 * half:4 * half + 4], src).then_inc(S["o_copied"], 1)
                add_output(S, 0, FULL, LAST)
                dve.wait_ge(S["added"], 1)

            peer(0)
            attention()
            peer(1)
            dve.wait_ge(gainf_in, 16)
            for t in range(TILES):
                n = P if t < FULL else LAST
                c.reset()
                peer_sems[1].wait(dve, "h_done", t + 1)
                c(dve.scalar_tensor_tensor(YSQ[0:n, :], H[0:n, t, :], 1.0, H[0:n, t, :], ALU.mult, ALU.mult,
                                           accum_out=rt[0:n, 0:1]))
                dve.tensor_scalar(rt[0:n, 0:1], rt[0:n, 0:1], 1.0 / D, EPS, ALU.mult, ALU.add).then_inc(last_ms, 1)
                dve.wait_ge(last_root, t + 1)
                rsqrt_refined(rt[0:n, 2:3], rt[0:n, 1:2], rt[0:n, 0:1], rt[0:n, 3:4])
                dve.scalar_tensor_tensor(H[0:n, t, :], H[0:n, t, :], rt[0:n, 2:3], GAINF[0:n, :], ALU.mult, ALU.mult)\
                   .then_inc(y_ready2, 1)

        @block.scalar
        def _(act):
            c = Chain(act, s_act)
            act.wait_ge(x_in, 16)
            for s in range(Q):
                c(act.activation(SQ[0:NC, :], X[0:NC, s, :], ACT.Square, accum_out=st[0:NC, 0, s:s + 1]))
            act.nop().then_inc(squares, 1)
            act.wait_ge(roots_in, 1)
            act.activation(st[0:NC, 2, :], st[0:NC, 1, :], ACT.Sqrt).then_inc(roots, 1)
            act.wait_ge(angles, 1)
            act.activation(w[:, 6:8, :], w[:, 4:6, :], ACT.Sin).then_inc(sines, 1)

            def turned_copy(r, out, src):
                act.wait_ge(turned, r + 1)
                act.copy(out, src).then_inc(turned_out, 1)

            for r, groups in enumerate(UR):
                n = len(groups)
                turned_copy(r, U[:, groups[0]:groups[0] + n, :].rearrange("p g n -> p (g n)"), ps[:, r % 4, 0:n * NC])
            for r, (ri, q0) in enumerate(WR):
                turned_copy(NU + r, WIN[:, q0:q0 + 4, :, ri, :],
                            ps[:, (NU + r) % 4, :].rearrange("p (q g n) -> p q g n", q=4, g=2))
            act.wait_ge(ca_ready, 2)
            for r, pairs in enumerate(VR):
                act.wait_ge(v_ready, r + 1)
                for g2 in range(2):
                    v_copy(act.copy, r, pairs, 0, g2).then_inc(v_act, 1)
            for r in range(PR):
                act.wait_ge(turned, NU + NW + r + 1)
                for g2 in range(2):
                    act.copy(M[0:GS, 8 * r + g2:8 * r + 8:2, :],
                             ps[0:GS, 4 + 2 * (r % 2) + g2, :].rearrange("p (q n) -> p q n", q=4)).then_inc(turned_out, 1)
            act.wait_ge(m_out, 16)
            for r in range(PR):
                act.wait_ge(y_ready, r + 1)
                for g2 in range(2):
                    z = Z[0:NC, :, 8 * GS * r:8 * GS * (r + 1)].rearrange("p t (q g j) -> p g q t j", g=2, j=GS)
                    act.activation(z[:, g2], ps[0:NC, 2 * (r % 4) + g2, :].rearrange("p (q t j) -> p q t j", q=4, j=GS),
                                   ACT.Gelu).then_inc(y_out, 1)
            for r in range(0, 2 * KT, 2):
                act.wait_ge(z_ready, r + 1)
                z_copy(act.copy, r).then_inc(z_act, 1)
            for t in range(TILES):
                n = P if t < FULL else LAST
                act.wait_ge(glu_ready, t + 1)
                if t >= 2:
                    act.wait_ge(mixed, t - 1)
                act.activation(SG[0:n, t % 2, :],
                               ps[0:n, 4 * (t % 2) + 2:4 * (t % 2) + 4, :].rearrange("p a b -> p (a b)"),
                               ACT.Sigmoid).then_inc(gate_ready, 1)

            def peer(L):
                S = peer_sems[L]

                def root(t):
                    S.wait(act, "ms_ready", t + 1)
                    act.activation(rt[:, 1:2], rt[:, 0:1], ACT.Sqrt).then_inc(S["root_ready"], 1)

                def xt_copy(t):
                    S.wait(act, "q_ready", 8 * t)
                    for i in range(2):
                        S.wait(act, "xt_ready", t + 1)
                        act.copy(XT[:, 4 * i:4 * i + 4, :].rearrange("p k n -> p (k n)"), ps[:, 2 + i, :])\
                           .then_inc(S["xt_copied"], 1)

                def q_copy(r, par):
                    S.wait(act, "q_ready", r + 1)
                    S.wait(act, "qt_ready", r - 1)
                    act.copy(QN[:, par, :], ps[:, 4 + par, 0:2 * P]).then_inc(S["q_copied"], 1)

                def qt_copy(r, par):
                    S.wait(act, "qt_ready", r + 1)
                    S.wait(act, "sc_ready", r - 1)
                    act.copy(QT[:, par].rearrange("p a n -> p (a n)"), ps[:, 6 + par, 0:2 * P]).then_inc(S["qt_copied"], 1)

                def sc_copy(r, par):
                    S.wait(act, "sc_ready", r + 1)
                    S.wait(act, "routed", r - 1)
                    act.copy(SC[:, par].rearrange("p a n -> p (a n)"), ps[:, 6 + par, 256:512]).then_inc(S["sc_copied"], 1)

                def exps(t):
                    S.wait(act, "fv_ready", t + 1)
                    flat = EXPS.rearrange("p h k -> p (h k)")
                    act.activation(flat, flat, ACT.Exp).then_inc(S["exp_done"], 1)

                def gelu(j, par):
                    S.wait(act, "dots", 16 * j + 16)
                    S.wait(act, "weights", j - 1)
                    act.activation(ge[:, par, :], hp[:, par, :], ACT.Gelu).then_inc(S["gelus"], 1)

                def diags(j, par, quarter):
                    rows = pe_rows(j)
                    n = len(rows) // 4
                    if quarter == 0:
                        S.wait(act, "weights", j + 1)
                    for i in range(quarter * n, quarter * n + n):
                        S.wait(act, "products", products_before(j) + i - 3)
                        act.activation(DIAG[:, i % 4, :], (ident if rows == PE_ROWS else fold)[:, :], ACT.Copy,
                                       scale=av[:, par, rows[i]:rows[i] + 1]).then_inc(S["diags"], 1)

                def slot(t, h, par, route, first_head, first):
                    j, r, m = t * 8 + h, t * 8 + h + 8, 1 - par
                    if route and first_head:
                        root(t + 1)
                    if not first:
                        gelu(j - 1, m)
                    if route and not first_head:
                        q_copy(r, par)
                    if not first:
                        diags(j - 1, m, 0)
                    if route and first_head:
                        xt_copy(t + 1)
                    if route and not first_head:
                        qt_copy(r, par)
                    if not first:
                        diags(j - 1, m, 1)
                    if route and first_head:
                        q_copy(r, par)
                    if route and not first_head:
                        sc_copy(r, par)
                    if not first:
                        diags(j - 1, m, 2)
                    if route and first_head:
                        qt_copy(r, par)
                    if not first:
                        diags(j - 1, m, 3)
                    if route and first_head:
                        sc_copy(r, par)

                def tile(t, route, first):
                    for par in range(2):
                        slot(t, par, par, route, par == 0, first and par == 0)
                    if route:
                        with act.Fori(1, HEADS // 2) as m:
                            for par in range(2):
                                slot(t, 2 * m + par, par, route, False, False)
                        exps(t + 1)
                    else:
                        for h in range(2, HEADS // 2):
                            slot(t, h, h % 2, route, False, False)

                root(0)
                xt_copy(0)
                def copies(m):
                    for par in range(2):
                        q_copy(2 * m + par, par)
                        qt_copy(2 * m + par, par)
                        sc_copy(2 * m + par, par)

                copies(0)
                with act.Fori(1, HEADS // 2) as m:
                    copies(m)
                exps(0)
                act.wait_ge(fold_in, 16)
                tile(0, True, True)
                with act.Fori(1, FULL) as t:
                    tile(t, True, False)
                tile(FULL, False, False)
                gelu(SLOTS - 1, 1)
                for quarter in range(4):
                    diags(SLOTS - 1, 1, quarter)

            def root_of(S, t):
                gate(act, S["ms"], t + 1)
                act.activation(rt[:, 1:2], rt[:, 0:1], ACT.Sqrt).then_inc(S["root"], 1)

            def xt_copies(S, t, which):
                gate(act, S["xt"], 2 * t + which + 1)
                for i in range(2):
                    act.copy((XKT, XQT)[which][:, 4 * i:4 * i + 4, :].rearrange("p k n -> p (k n)"), ps[:, i, :])\
                       .then_inc(S["xt_copied"], 1)

            def kv_copy(S, t):
                gate(act, S["kv"], t + 1)
                act.copy(KVN, ps[:, 2, 0:2 * P]).then_inc(S["kv_copied"], 1)

            def q_copy(S, t):
                gate(act, S["q"], t + 1)
                act.copy(QNA, ps[:, 4:6, :].rearrange("p a b -> p (a b)")).then_inc(S["q_copied"], 1)

            def qt_copy(S, t):
                gate(act, S["qt"], t + 1)
                act.copy(QTA.rearrange("p i n -> p (i n)"), ps[:, 6:8, :].rearrange("p a b -> p (a b)"))\
                   .then_inc(S["qt_copied"], 1)

            def att_project(S, t):
                xt_copies(S, t, 0)
                kv_copy(S, t)
                act.copy(V2[:, 1, :], ps[:, 2, P:2 * P]).then_inc(S["kv_copied"], 1)
                xt_copies(S, t, 1)
                q_copy(S, t)

            def att_exps(S, t, rows, n, between=()):
                for step in between[:1]:
                    step()
                gate(act, S["max"], t + 1)
                act.activation(mx[:, 3, 0:n], mx[:, 1, 0:n], ACT.Exp)
                for i in range(n):
                    last = act.activation(rows[:, i, :], rows[:, i, :], ACT.Exp, bias=mx[:, 0, i:i + 1],
                                          accum_out=mx[:, 2, i:i + 1])
                    if i == n - 1:
                        last.then_inc(S["exps"], 1)
                    if i % 4 == 3:
                        for step in between[1 + i // 4:2 + i // 4]:
                            step()

            def att_tile(t, more):
                S = att_sems[0]
                rows = PB.rearrange("p a b n -> p (a b) n")
                if more:
                    att_exps(S, t, rows, QH, (lambda: xt_copies(S, t + 1, 0), lambda: kv_copy(S, t + 1),
                                              lambda: xt_copies(S, t + 1, 1)))
                    root_of(S, t + 2)
                    q_copy(S, t + 1)
                    qt_copy(S, t + 1)
                else:
                    act.wait_ge(win_out, 48)
                    att_exps(S, t, rows, QH, (lambda: xt_copies(S, FULL, 0), lambda: kv_copy(S, FULL),
                                              lambda: xt_copies(S, FULL, 1)))
                    q_copy(S, FULL)
                for r in range(0, QPK, 2):
                    gate(act, S["pt"], QPK * t + r + 1)
                    pt_copy(act.copy, r).then_inc(S["pt_act"], 1)
                gate(act, S["o"], t + 1)
                gate(act, S["kv_copied"], 2 * t + 3)
                act.copy(V2[:, 0, :], V2[:, 1, :]).then_inc(S["v_moved"], 1)
                gate(act, S["v_moved"], t + 1)
                act.copy(V2[:, 1, :], KVN[:, P:2 * P]).then_inc(S["kv_copied"], 1)

            def attention():
                root_of(att_sems[0], 0)
                att_project(att_sems[0], 0)
                root_of(att_sems[0], 1)
                qt_copy(att_sems[0], 0)
                att_tile(0, True)
                with act.Fori(1, FULL - 1) as t:
                    att_tile(t, True)
                att_tile(FULL - 1, False)
                S = att_sems[1]
                act.wait_ge(S["pt"], 1)
                act.copy(KBT.rearrange("p b n -> p (b n)"), ps[:, 0:2, :].rearrange("p a b -> p (a b)"))\
                   .then_inc(S["pt_act"], 1)
                att_exps(S, 0, SB, NSEQ)
                act.wait_ge(S["pt"], 2)
                act.copy(PTB.rearrange("p b n -> p (b n)"), ps[:, 4:6, :].rearrange("p a b -> p (a b)"))\
                   .then_inc(S["pt_act"], 1)
                act.wait_ge(S["pt"], 3)
                act.copy(PTN[0:LAST].rearrange("p b n -> p (b n)"), ps[0:LAST, 6:8, :].rearrange("p a b -> p (a b)"))\
                   .then_inc(S["pt_act"], 1)

            peer(0)
            attention()
            peer(1)
            for t in range(TILES):
                n = P if t < FULL else LAST
                act.wait_ge(last_ms, t + 1)
                act.activation(rt[0:n, 1:2], rt[0:n, 0:1], ACT.Sqrt).then_inc(last_root, 1)

        @block.tensor
        def _(pe):
            pe.wait_ge(ident_in, 16)
            pe.wait_ge(normed, Q)
            for r, groups in enumerate(UR):
                if r >= 4:
                    pe.wait_ge(turned_out, r - 3)
                for i, g in enumerate(groups):
                    mm = pe.transpose(ps[:, r % 4, i * NC:(i + 1) * NC], XN[0:NC, g, :, :].rearrange("p s j -> p (s j)"), ident[0:NC, 0:NC])
                mm.then_inc(turned, 1)
            for r, (ri, q0) in enumerate(WR):
                n = NU + r
                pe.wait_ge(e_ready, ri + 1)
                pe.wait_ge(turned_out, n - 3)
                for i in range(4):
                    mm = pe.transpose(ps[:, n % 4, i * P:(i + 1) * P], E[:, ri, q0 + i, :], ident[:, :])
                mm.then_inc(turned, 1)
            pe.wait_ge(turned_out, NU + NW)
            for r, pairs in enumerate(VR):
                if r >= 4:
                    pe.wait_ge(v_act, 2 * (r - 3))
                    pe.wait_ge(v_dve, 2 * (r - 3))
                half = len(pairs) // 2
                for i, q in enumerate(pairs):
                    for g2 in range(2):
                        b, j = 2 * (r % 4) + i // half, 2 * (i % half) + g2
                        mm = pe.matmul(ps[:, b, j * NC:(j + 1) * NC],
                                       WIN[:, q, g2, :, :].rearrange("p r n -> p (r n)"), U[:, 2 * q + g2, :],
                                       start=True, stop=True)
                mm.then_inc(v_ready, 1)
            pe.wait_ge(ca_ready, 2)
            pe.wait_ge(v_act, 2 * len(VR))
            pe.wait_ge(v_dve, 2 * len(VR))
            for r in range(PR):
                if r >= 2:
                    pe.wait_ge(turned_out, NU + NW + 2 * (r - 1))
                for i in range(8):
                    q, g2 = 4 * r + i // 2, i % 2
                    rows = slice(SD * g2, SD * g2 + SD)
                    out = ps[0:GS, 4 + 2 * (r % 2) + g2, (i // 2) * BLK:(i // 2 + 1) * BLK]
                    for ri in range(2):
                        mm = pe.matmul(out, Bb[rows, ri, q, :],
                                       CA[rows, ri, q, 0:Q, :].rearrange("p s j -> p (s j)"),
                                       start=(ri == 0), stop=(ri == 1))
                mm.then_inc(turned, 1)
            pe.wait_ge(k_in, 16 * Q)
            pe.wait_ge(turned_out, NU + NW + 2 * PR)

            def within_chunks(r):
                for i in range(8):
                    out = ps[0:NC, 2 * (r % 4) + i % 2, (i // 2) * BLK:(i // 2 + 1) * BLK]
                    pe.matmul(out, U[:, 8 * r + i, :], K[:, 8 * r + i, :], start=(i < 2), stop=False,
                              skip_group_check=True)

            for r in range(4):
                within_chunks(r)
            pe.wait_ge(scanned, 1)
            for r in range(PR):
                if r >= 4:
                    pe.wait_ge(y_out, 2 * (r - 3))
                    within_chunks(r)
                for i in range(8):
                    q, g2 = 4 * r + i // 2, i % 2
                    rows = slice(SD * g2, SD * g2 + SD)
                    out = ps[0:NC, 2 * (r % 4) + g2, (i // 2) * BLK:(i // 2 + 1) * BLK]
                    for ri in range(2):
                        mm = pe.matmul(out, HP[rows, ri, q, :],
                                       CA[rows, ri, q, 1:Q + 1, :].rearrange("p s j -> p (s j)"),
                                       start=False, stop=(ri == 1), skip_group_check=True)
                mm.then_inc(y_ready, 1)
            pe.wait_ge(y_out, 2 * PR)
            for r in range(2 * KT):
                kt, half = r // 2, r % 2
                if r >= 4:
                    pe.wait_ge(z_act if r % 2 == 0 else z_dve, (r - 4) // 2 + 1)
                for i in range(4):
                    mm = pe.transpose(ps[:, r % 4, i * NC:(i + 1) * NC],
                                      Z[0:NC, 4 * half + i, kt * P:(kt + 1) * P], ident[0:NC, 0:NC])
                mm.then_inc(z_ready, 1)
            pe.wait_ge(z_act, KT)
            pe.wait_ge(z_dve, KT)
            pe.wait_ge(glu_in, 32)
            for t in range(TILES):
                n = P if t < FULL else LAST
                if t >= 2:
                    pe.wait_ge(mixed, t - 1)
                for b in range(4):
                    for kt in range(KT):
                        mm = pe.matmul(ps[0:n, 4 * (t % 2) + b, :], ZT[:, kt, t * P:t * P + n],
                                       WGLU[:, kt, 512 * b:512 * (b + 1)], start=(kt == 0), stop=(kt == KT - 1))
                mm.then_inc(glu_ready, 1)

            def peer(L):
                S = peer_sems[L]

                def xt(t):
                    S.wait(pe, "x_ready", t + 1)
                    S.wait(pe, "xt_copied", 2 * t)
                    for k in range(KT):
                        mm = pe.transpose(ps[:, 2 + k // 4, (k % 4) * P:(k % 4 + 1) * P], XNEXT[:, k * P:(k + 1) * P],
                                          ident[:, :])
                    mm.then_inc(S["xt_ready"], 1)

                def queries(t, h, par):
                    r = 8 * t + h
                    S.wait(pe, "xt_copied", 2 * t + 2)
                    S.wait(pe, "q_copied", r - 1)
                    for k in range(KT):
                        mm = pe.matmul(ps[:, 4 + par, 0:2 * P], XT[:, k, :],
                                       WQ[k // 4][:, k % 4, bass.ds(h * 2 * P, 2 * P)], start=(k == 0), stop=(k == KT - 1))
                    mm.then_inc(S["q_ready"], 1)

                def turn_queries(r, par):
                    S.wait(pe, "q_copied", r + 1)
                    S.wait(pe, "sc_copied", r - 1)
                    for i in range(2):
                        mm = pe.transpose(ps[:, 6 + par, i * P:(i + 1) * P], QN[:, par, i * P:(i + 1) * P], ident[:, :])
                    mm.then_inc(S["qt_ready"], 1)

                def scores(r, h, par):
                    S.wait(pe, "qt_copied", r + 1)
                    for i in range(2):
                        mm = pe.matmul(ps[:, 6 + par, 256 + i * P:256 + (i + 1) * P], QT[:, par, i, :],
                                       KEYS[:, bass.ds(2 * h + i, 1), :].rearrange("p a n -> p (a n)"),
                                       start=True, stop=True)
                    mm.then_inc(S["sc_ready"], 1)

                def products(t, j, quarter, starts):
                    rows = pe_rows(j)
                    n = len(rows) // 4
                    if starts and quarter == 0:
                        S.wait(pe, "h_done", t)
                    for i in range(quarter * n, quarter * n + n):
                        k = rows[i]
                        S.wait(pe, "diags", products_before(j) + i + 1)
                        gate(pe, v_in[k % NV_RING], 16 * (2 * j + k // NV_RING + 1) + L * 16 * 2 * SLOTS)
                        for half in range(2):
                            mm = pe.matmul(ps[:, half, :], DIAG[:, i % 4, :],
                                           VROWS[k % NV_RING][:, half * 512:(half + 1) * 512],
                                           start=(starts and i == 0), stop=False, skip_group_check=True)
                        mm.then_inc(S["products"], 1)

                def slot(t, h, par, route, first_head, first, second):
                    j, r = t * 8 + h, t * 8 + h + 8
                    if route and not first_head:
                        queries(t + 1, h, par)
                    if not first:
                        products(t, j - 1, 0, second)
                    if route and first_head:
                        xt(t + 1)
                    if route and not first_head:
                        turn_queries(r, par)
                    if not first:
                        products(t, j - 1, 1, second)
                    if route and first_head:
                        queries(t + 1, h, par)
                    if route and not first_head:
                        scores(r, h, par)
                    if not first:
                        products(t, j - 1, 2, second)
                    if route and first_head:
                        turn_queries(r, par)
                    if not first:
                        products(t, j - 1, 3, second)
                    if route and first_head:
                        scores(r, h, par)

                def tile(t, route, first):
                    for par in range(2):
                        slot(t, par, par, route, par == 0, first and par == 0, par == 1)
                    if route:
                        with pe.Fori(1, HEADS // 2) as m:
                            for par in range(2):
                                slot(t, 2 * m + par, par, route, False, False, False)
                    else:
                        for h in range(2, HEADS // 2):
                            slot(t, h, h % 2, route, False, False, False)

                pe.wait_ge(mixed, TILES)
                xt(0)
                pe.wait_ge(wq_in, 48 * (L + 1))
                def route_pair(m):
                    for par in range(2):
                        queries(0, 2 * m + par, par)
                        turn_queries(2 * m + par, par)
                        scores(2 * m + par, 2 * m + par, par)

                route_pair(0)
                with pe.Fori(1, HEADS // 2) as m:
                    route_pair(m)
                tile(0, True, True)
                with pe.Fori(1, FULL) as t:
                    tile(t, True, False)
                tile(FULL, False, False)
                for quarter in range(4):
                    products(FULL, SLOTS - 1, quarter, False)

            def att_project(S, t):
                gate(pe, S["added"], t - 1)
                for which, (x, xt, out, w) in enumerate(((XK, XKT, ps[:, 2:3, 0:2 * P], WKV), (XQ, XQT, ps[:, 4:6, :], WQA))):
                    gate(pe, S["x"], 2 * t + which + 1)
                    if which == 1:
                        gate(pe, S["xt_copied"], 4 * t + 2)
                    for k in range(KT):
                        mm = pe.transpose(ps[:, k // 4, (k % 4) * P:(k % 4 + 1) * P], x[:, k * P:(k + 1) * P], ident[:, :])
                    mm.then_inc(S["xt"], 1)
                    gate(pe, S["xt_copied"], 4 * t + 2 * which + 2)
                    n = out.shape[2]
                    for b in range(out.shape[1]):
                        for k in range(KT):
                            mm = pe.matmul(out[:, b, :], xt[:, k, :], w[:, k, b * n:(b + 1) * n],
                                           start=(k == 0), stop=(k == KT - 1))
                    mm.then_inc(S["q"] if which else S["kv"], 1)
                    if which == 0:
                        gate(pe, S["kv_copied"], 2 * t + 1)
                        pe.transpose(ps[:, 3, 0:P], KVN[:, 0:P], ident[:, :]).then_inc(S["kt"], 1)
                gate(pe, S["q_copied"], t + 1)
                for i in range(QPK):
                    mm = pe.transpose(ps[:, 6 + i // 4, (i % 4) * P:(i % 4 + 1) * P], QNA[:, i * P:(i + 1) * P], ident[:, :])
                mm.then_inc(S["qt"], 1)

            def att_output(S, t, n, copied):
                gate(pe, S["o_copied"], copied)
                for b in range(2):
                    for i in range(QPK):
                        mm = pe.matmul(ps[0:n, 4 + b, :], OT[:, i, 0:n], WO[:, i, b * 512:(b + 1) * 512],
                                       start=(i == 0), stop=(i == QPK - 1))
                mm.then_inc(S["y"], 1)

            def att_tile(t, more):
                S = att_sems[0]
                gate(pe, S["qt_copied"], t + 1)
                gate(pe, S["kt_copied"], 2 * t + 2)
                for i in range(QPK):
                    if i >= 4:
                        gate(pe, S["masked"], QPK * t + i - 3)
                    pe.matmul(ps[:, i % 4, :], QTA[:, i, :], KZ[:, :, bass.ds(t * P, 2 * P)],
                              start=True, stop=True).then_inc(S["s"], 1)
                gate(pe, S["masked"], QPK * t + QPK)
                att_project(S, t + 1)
                if more:
                    gate(pe, S["qt_copied"], t + 2)
                    gate(pe, S["kt_copied"], 2 * t + 4)
                else:
                    pe.wait_ge(att_sems[1]["kt_copied"], 1)
                    pe.wait_ge(sample_q, 4)
                gate(pe, S["probs"], t + 1)
                for r in range(QPK):
                    for half in range(2):
                        for kvh in range(KVH):
                            at = (2 * half + kvh) * P
                            mm = pe.transpose(ps[:, r, at:at + P], PB[:, r, kvh, half * P:(half + 1) * P], ident[:, :])
                    mm.then_inc(S["pt"], 1)
                gate(pe, S["pt_act"], 4 * t + 4)
                gate(pe, S["pt_dve"], 4 * t + 4)
                gate(pe, S["kv_copied"], 2 * t + 2)
                for r in range(QPK // 2):
                    for half in range(2):
                        mm = pe.matmul(ps[:, r, :], V2[:, half, :],
                                       PT[:, half, 2 * r:2 * r + 2].rearrange("p i k n -> p (i k n)"),
                                       start=(half == 0), stop=(half == 1))
                mm.then_inc(S["o"], 1)
                att_output(S, t, P, 2 * t + 2)

            def attention():
                att_project(att_sems[0], 0)
                att_tile(0, True)
                with pe.Fori(1, FULL - 1) as t:
                    att_tile(t, True)
                att_tile(FULL - 1, False)
                S = att_sems[1]
                pe.wait_ge(att_sems[0]["added"], FULL)
                pe.wait_ge(buf_in, 32)
                for b in range(NSEQ):
                    mm = pe.transpose(ps[:, b // 4, (b % 4) * P:(b % 4 + 1) * P], KBUF[:, b, :], ident[:, :])
                mm.then_inc(S["pt"], 1)
                pe.wait_ge(S["pt_act"], 1)
                for r in range(NSEQ // 2):
                    for b in range(2):
                        q = QBD[:, 2 * r + b, :]
                        pe.matmul(ps[:, r, b * WIDE:b * WIDE + P], q, KBT[:, 2 * r + b, :], start=True, stop=True)
                        mm = pe.matmul(ps[:, r, b * WIDE + P:(b + 1) * WIDE], q, KNT, start=True, stop=True)
                    mm.then_inc(S["s"], 1)
                pe.wait_ge(S["probs"], 1)
                for b in range(NSEQ):
                    mm = pe.transpose(ps[:, 4 + b // 4, (b % 4) * P:(b % 4 + 1) * P], SB[:, b, 0:P], ident[:, :])
                mm.then_inc(S["pt"], 1)
                for b in range(NSEQ):
                    mm = pe.transpose(ps[0:LAST, 6 + b // 4, (b % 4) * P:(b % 4 + 1) * P], SB[:, b, P:WIDE], ident[:, :])
                mm.then_inc(S["pt"], 1)
                pe.wait_ge(S["pt_act"], 3)
                pe.wait_ge(att_sems[0]["kv_copied"], 2 * FULL + 2)
                for b in range(NSEQ):
                    out = ps[:, 4 + b // 4, (b % 4) * P:(b % 4 + 1) * P]
                    pe.matmul(out, VBUF[:, b, :], PTB[:, b, :], start=True, stop=False)
                    mm = pe.matmul(out, V2[0:LAST, 1, :], PTN[0:LAST, b, :], start=False, stop=True)
                mm.then_inc(S["o"], 1)
                att_output(S, 0, LAST, 4)
                pe.wait_ge(S["added"], 1)

            peer(0)
            attention()
            peer(1)

        @block.gpsimd
        def _(pool):
            c = Chain(pool, s_pool)
            pool.wait_ge(bc_in, 64)
            pool.wait_ge(normed, Q)
            pool.wait_ge(powers_ready, 1)
            tC = TMPC.rearrange("p (q s j) -> p q s j", s=Q + 1, j=GS)
            c(pool.tensor_tensor(CA[:, 0], powers(pw, 0, Q + 1), over(CRAW[:, 0], Q + 1), ALU.mult))
            c(pool.tensor_tensor(tC, powers(pw, 1, Q + 1), over(CRAW[:, 1], Q + 1), ALU.mult))
            flat = CA[:, 0].rearrange("p q s j -> p (q s j)")
            pool.tensor_tensor(flat, flat, TMPC, ALU.subtract).then_inc(ca_ready, 1)
            pool.wait_ge(turned, NU + NW)
            pool.wait_ge(ident_in, 16)
            c(pool.tensor_tensor(SKIP, ident[0:GS, 0:GS].unsqueeze(1).to_broadcast([GS, G, GS]),
                                 dsk.unsqueeze(2).to_broadcast([GS, G, GS]), ALU.mult))
            pool.wait_ge(turned_out, NU + NW + 2 * PR)
            pool.tensor_tensor(M[0:GS, :, 0:GS], M[0:GS, :, 0:GS], SKIP, ALU.add).then_inc(skip_added, 1)

            def peer(L):
                S = peer_sems[L]
                tab_u, tab_v = io[f"peer_u{L}"], io[f"peer_v{L}"]

                def gather_u(j, par, k):
                    S.wait(pool, "dots", 16 * j + k + 1 - NU_RING)
                    pool.indirect_dma_start(UROWS[:, k % NU_RING, :], None, tab_u,
                                            bass.IndirectOffsetOnAxis(ap=idxu[:, par, k:k + 1], axis=0))\
                        .then_inc(u_in[k % NU_RING], 16)

                def gather_v(j, par, k):
                    before, k_before = (j, k - NV_RING) if k >= NV_RING else (j - 1, k - NV_RING + TOPK)
                    rows = pe_rows(before)
                    if k_before in rows:
                        S.wait(pool, "products", products_before(before) + rows.index(k_before) + 1)
                    else:
                        S.wait(pool, "rows_added", len(DVE_ROWS) * before + DVE_ROWS.index(k_before) + 1)
                    pool.indirect_dma_start(VROWS[k % NV_RING], None, tab_v,
                                            bass.IndirectOffsetOnAxis(ap=idxv[:, par, k:k + 1], axis=0))\
                        .then_inc(v_in[k % NV_RING], 16)

                def slot(t, h, par):
                    j = t * 8 + h
                    S.wait(pool, "idxu_ready", j + 1)
                    S.wait(pool, "idxv_ready", j)
                    for k in range(TOPK):
                        gather_u(j, par, k)
                        gather_v(j - 1, 1 - par, k)

                def first_slots():
                    S.wait(pool, "idxu_ready", 1)
                    for k in range(NU_RING):
                        gather_u(0, 0, k)
                    S.wait(pool, "idxv_ready", 1)
                    for k in range(NV_RING):
                        gather_v(0, 0, k)
                    for k in range(NU_RING, TOPK):
                        gather_u(0, 0, k)
                    S.wait(pool, "idxu_ready", 2)
                    for k in range(TOPK):
                        gather_u(1, 1, k)
                        if k % 2:
                            gather_v(0, 0, NV_RING + k // 2)

                def tile(t, route, first):
                    if first:
                        first_slots()
                    else:
                        for par in range(2):
                            slot(t, par, par)
                    if route:
                        with pool.Fori(1, HEADS // 2) as m:
                            for par in range(2):
                                slot(t, 2 * m + par, par)
                    else:
                        for h in range(2, HEADS // 2):
                            slot(t, h, h % 2)

                tile(0, True, True)
                with pool.Fori(1, FULL) as t:
                    tile(t, True, False)
                tile(FULL, False, False)
                S.wait(pool, "idxv_ready", SLOTS)
                for k in range(TOPK):
                    gather_v(SLOTS - 1, 1, k)

            peer(0)
            pool.wait_ge(att_sems[1]["added"], 1)
            peer(1)


def _laid_out(inp):
    import numpy as np

    def states(a):
        a = np.moveaxis(a.reshape(*a.shape[:-2], PAIRS, 2, SD), (-2, -1), (0, 1))
        return a.reshape(P, *a.shape[2:])

    f = {k: np.asarray(v) for k, v in inp.items()}
    x = np.concatenate([f["x_prompt"].reshape(SEQ, D), f["x_sample"].reshape(TOK - SEQ, D)])
    lam = [f["ssm_lam_re"][0], f["ssm_lam_im"][0], np.broadcast_to(f["ssm_log_dt"][0][:, None], (G, SD))]
    row, col = np.arange(P)[:, None], np.arange(2 * P)[None, :]
    seen = (row + P - col >= 0) & (row + P - col < P)
    masks = np.concatenate([np.where(seen & (col >= P), 0.0, NEG), np.where(seen, 0.0, NEG)], 1).astype(np.float32)
    step, b, col = (row % STEPS)[:, :, None], np.arange(NSEQ)[None, :, None], np.arange(WIDE)[None, None, :]
    new = col - P
    seen = np.where(new < 0, step + P - col < P, (new // STEPS == b) & (new % STEPS <= step))
    smask = np.where(seen, 0.0, NEG).astype(np.float32)
    out = {
        "x": x,
        "ident": np.eye(P, dtype=np.float32),
        "fold": np.tile(np.eye(LAST, dtype=np.float32), (2, 2)),
        "gains": np.concatenate([f["norm_mix"], f["norm_ffn"], f["norm_kv"][None], f["norm_final"][None]]),
        "s5par": np.stack([states(a) for a in lam], 1),
        "s5b": np.stack([states(f[n][0].transpose(2, 0, 1)).transpose(0, 2, 1) for n in ("ssm_b_re", "ssm_b_im")], 1),
        "s5c": np.stack([states(f[n][0].transpose(1, 0, 2)).transpose(0, 2, 1) for n in ("ssm_c_re", "ssm_c_im")], 1),
        "h0": np.stack([states(f[n][0]) for n in ("state_ssm_re", "state_ssm_im")], 1),
        "dskip": f["ssm_d"][0].reshape(G, GS).T,
        "w_glu": f["ssm_w_glu"][0],
        "iota": np.broadcast_to(np.arange(TOPK, dtype=np.float32), (P, TOPK)),
        "peer_wq": f["peer_w_q"],
        "w_q": f["w_q"][0].reshape(D, KVH, QPK, HD).transpose(0, 2, 1, 3).reshape(D, D),
        "w_o": f["w_o"][0].reshape(KVH, QPK, HD, D).transpose(1, 0, 2, 3).reshape(D, D),
        "w_kv": f["w_kv"],
        "k_buf": f["cache_k_win"].reshape(NSEQ, P, KVH * HD),
        "v_buf": f["cache_v_win"].reshape(NSEQ, P, KVH * HD),
        "masks": masks, "smask": smask,
        "sinks": np.concatenate([np.broadcast_to(f["attn_sinks"][0].reshape(KVH, QPK).T.reshape(1, QH), (P, QH)),
                                 np.repeat(f["attn_sinks"][0], STEPS)[:, None]], 1),
        "keys": f["peer_sub_keys"].transpose(0, 4, 1, 2, 3).reshape(2, P, 2 * HEADS, NKEY),
        "peer_u0": f["peer_u"][0], "peer_u1": f["peer_u"][1],
        "peer_v0": f["peer_v"][0], "peer_v1": f["peer_v"][1],
    }
    return {k: np.ascontiguousarray(v) for k, v in out.items()}


_OUTS = {"hs": (P, 2, NSEQ, PAIRS), "hf": (P, 2, PAIRS), "y": (TOK, D), "kv_p": (P, 2 * P), "kv_s": (2, NSEQ, P, P)}
_SCRATCH = {"kern": (G, GS, (2 * Q - 1) * GS)}


def kernel(**inputs):
    import numpy as np
    import concourse.bacc as bacc
    from concourse.bass_utils import run_bass_kernel_spmd

    nc = bacc.Bacc("TRN2", target_bir_lowering=False, num_devices=1)
    arrays = {f"in_{k}": v for k, v in _laid_out(inputs).items()}
    io = {k[3:]: nc.dram_tensor(k, v.shape, mybir.dt.from_np(v.dtype), kind="ExternalInput").ap()
          for k, v in arrays.items()}
    for k, shape in _OUTS.items():
        io[k] = nc.dram_tensor(f"out_{k}", shape, F32, kind="ExternalOutput").ap()
    for k, shape in _SCRATCH.items():
        io[k] = nc.dram_tensor(k, shape, F32, kind="Internal").ap()
    build(nc, io)
    got = run_bass_kernel_spmd(nc, [arrays], core_ids=[0]).results[0]

    def groups(a):
        a = np.moveaxis(a.reshape(2, SD, *a.shape[1:]), (0, 1), (-2, -1))
        return a.reshape(*a.shape[:-3], G, SD)

    hs, hf, y, kvp, kvs = (got[f"out_{k}"] for k in ("hs", "hf", "y", "kv_p", "kv_s"))
    return (y[:SEQ].reshape(1, SEQ, D), y[SEQ:].reshape(NSEQ, STEPS, D),
            groups(hf[:, 0])[None, None], groups(hf[:, 1])[None, None],
            kvp[:, :P].reshape(1, P, KVH, HD), kvp[:, P:].reshape(1, P, KVH, HD),
            groups(hs[:, 0])[None], groups(hs[:, 1])[None],
            kvs[0].reshape(NSEQ, P, KVH, HD), kvs[1].reshape(NSEQ, P, KVH, HD))
```
